# Optimizing a Trainium2 kernel written in Bass

```python
import math
import jax, jax.numpy as jnp
from jax import lax
import numpy as np

D_MODEL = 1024
BATCH = 1
SEQ = 512
DEPTH = 2

CHUNK = 64
EPS = 1e-6
N_EVEN = (DEPTH + 1) // 2
N_ODD = DEPTH // 2

A_WIDTH = 512
A_BLOCKS = 8
A_BLOCK = A_WIDTH // A_BLOCKS
CONV_WIDTH = 4
RG_C = 8.0
B_HEADS = 8
B_HEAD_DIM = 64
B_WIDTH = B_HEADS * B_HEAD_DIM
LEFT_CHUNKS = 8
BAND = LEFT_CHUNKS + 1
REL_CLIP = 256
AB_IN = 2 * A_WIDTH + 3 * B_WIDTH
AB_MIX = A_WIDTH + B_WIDTH
C_HEADS = 8
C_DK = 128
C_DV = 128
C_WIDTH = C_HEADS * C_DK
C_IN = 2 * C_HEADS * C_DK + 2 * C_HEADS * C_DV
N_GROUPS = 4
EXPERTS_PER_GROUP = 8
N_EXPERTS = N_GROUPS * EXPERTS_PER_GROUP
TOP_K = 2
D_EXPERT = 512
MOE_BLOCK = 128

kernel_name = "hybrid_rglru_chunkattn_hgrn2_hmoe"

def rms_norm(x, g):
    xf = x.astype(jnp.float32)
    y = xf * lax.rsqrt(jnp.mean(xf * xf, axis=-1, keepdims=True) + EPS)
    return (y * g.astype(jnp.float32)).astype(x.dtype)

def causal_depthwise_conv(x, w, b):
    S = x.shape[1]
    xp = jnp.pad(x, ((0, 0), (CONV_WIDTH - 1, 0), (0, 0)))
    y = b
    for j in range(CONV_WIDTH):
        y = y + w[j] * xp[:, j:j + S]
    return y

def rg_lru(x, w_a, b_a, w_x, b_x, lam):
    B_, S, _ = x.shape
    xb = x.reshape(B_, S, A_BLOCKS, A_BLOCK)
    r = jax.nn.sigmoid((jnp.einsum('bsnc,ncd->bsnd', xb, w_a).reshape(B_, S, A_WIDTH) + b_a).astype(jnp.float32))
    i = jax.nn.sigmoid((jnp.einsum('bsnc,ncd->bsnd', xb, w_x).reshape(B_, S, A_WIDTH) + b_x).astype(jnp.float32))
    log_a = RG_C * r * jax.nn.log_sigmoid(lam.astype(jnp.float32))
    a = jnp.exp(log_a)
    u = jnp.sqrt(-jnp.expm1(2.0 * log_a)) * (i * x.astype(jnp.float32))

    def combine(left, right):
        a1, b1 = left
        a2, b2 = right
        return a1 * a2, a2 * b1 + b2

    _, h = lax.associative_scan(combine, (a, u), axis=1)
    return h.astype(x.dtype)

def chunked_rel_attention(q, k, v, rel_bias):
    B_, S = q.shape[:2]
    NC = S // CHUNK
    qc = q.reshape(B_, NC, CHUNK, B_HEADS, B_HEAD_DIM)
    band_idx = jnp.arange(NC)[:, None] + jnp.arange(BAND)[None, :]

    def gather_band(t):
        tc = t.reshape(B_, NC, CHUNK, B_HEADS, B_HEAD_DIM)
        tp = jnp.pad(tc, ((0, 0), (LEFT_CHUNKS, 0), (0, 0), (0, 0), (0, 0)))
        return tp[:, band_idx].reshape(B_, NC, BAND * CHUNK, B_HEADS, B_HEAD_DIM)

    kb = gather_band(k)
    vb = gather_band(v)
    qpos = jnp.arange(CHUNK)
    kpos = ((jnp.arange(BAND)[:, None] - LEFT_CHUNKS) * CHUNK + jnp.arange(CHUNK)[None, :]).reshape(-1)
    rel = jnp.clip(qpos[:, None] - kpos[None, :], -REL_CLIP, REL_CLIP) + REL_CLIP
    bias = rel_bias[:, rel].astype(jnp.float32)
    valid = (jnp.arange(NC)[:, None] - LEFT_CHUNKS + jnp.arange(BAND)[None, :]) >= 0
    valid = jnp.repeat(valid, CHUNK, axis=1)
    s = jnp.einsum('bcihd,bckhd->bchik', qc, kb, preferred_element_type=jnp.float32) * (B_HEAD_DIM ** -0.5)
    s = s + bias[None, None]
    s = jnp.where(valid[None, :, None, None, :], s, -1e30)
    p = jax.nn.softmax(s, axis=-1)
    o = jnp.einsum('bchik,bckhd->bcihd', p.astype(v.dtype), vb)
    return o.reshape(B_, S, B_WIDTH)

def mixer_ab(h, w_in, conv_w, conv_b, w_a, b_a, w_x, b_x, lam, rel_bias, w_out):
    B_, S = h.shape[:2]
    z = h @ w_in
    xa, ga, q, k, v = jnp.split(z, [A_WIDTH, 2 * A_WIDTH, 2 * A_WIDTH + B_WIDTH, 2 * A_WIDTH + 2 * B_WIDTH], axis=-1)
    ya = rg_lru(causal_depthwise_conv(xa, conv_w, conv_b), w_a, b_a, w_x, b_x, lam) * jax.nn.gelu(ga)
    hs = (B_, S, B_HEADS, B_HEAD_DIM)
    yb = chunked_rel_attention(q.reshape(hs), k.reshape(hs), v.reshape(hs), rel_bias)
    return jnp.concatenate([ya, yb], axis=-1) @ w_out

def hgrn2_mixer(h, w_in, lb, norm_g, w_out):
    B_, S = h.shape[:2]
    NC = S // CHUNK
    f32 = jnp.float32
    z = h @ w_in
    q, fz, i, g = jnp.split(z, [C_HEADS * C_DK, 2 * C_HEADS * C_DK, 2 * C_HEADS * C_DK + C_HEADS * C_DV], axis=-1)
    lbf = lb.astype(f32)
    f = lbf + (1.0 - lbf) * jax.nn.sigmoid(fz.astype(f32))
    log_f = jnp.log(f)
    kk = 1.0 - f
    q = jax.nn.silu(q.astype(f32))

    def heads(t, d):
        return t.astype(f32).reshape(B_, NC, CHUNK, C_HEADS, d).transpose(1, 0, 3, 2, 4)

    qc, kc, lfc, vc = heads(q, C_DK), heads(kk, C_DK), heads(log_f, C_DK), heads(i, C_DV)
    causal = jnp.tril(jnp.ones((CHUNK, CHUNK), dtype=bool))

    def step(state, inp):
        qj, kj, lfj, vj = inp
        b = jnp.cumsum(lfj, axis=-2)
        diff = b[..., :, None, :] - b[..., None, :, :]
        decay = jnp.exp(jnp.where(causal[:, :, None], diff, -jnp.inf))
        attn = jnp.einsum('bhtk,bhsk,bhtsk->bhts', qj, kj, decay)
        o = jnp.einsum('bhts,bhsv->bhtv', attn, vj) + jnp.einsum('bhtk,bhkv->bhtv', qj * jnp.exp(b), state)
        b_last = b[..., -1:, :]
        new_state = jnp.exp(b_last[..., 0, :])[..., None] * state + jnp.einsum('bhsk,bhsv->bhkv', kj * jnp.exp(b_last - b), vj)
        return new_state, o

    s0 = jnp.zeros((B_, C_HEADS, C_DK, C_DV), f32)
    _, o = lax.scan(step, s0, (qc, kc, lfc, vc))
    o = o.transpose(1, 0, 3, 2, 4).reshape(B_, S, C_HEADS, C_DV)
    o = o * lax.rsqrt(jnp.mean(o * o, axis=-1, keepdims=True) + EPS)
    o = o.reshape(B_, S, C_HEADS * C_DV) * norm_g.astype(f32) * jax.nn.silu(g.astype(f32))
    return o.astype(h.dtype) @ w_out

def hier_moe(h, router_group, router_expert, w_gate, w_up, w_down):
    B_, S, D = h.shape
    T = B_ * S
    f32 = jnp.float32
    xt = h.reshape(T, D)
    g_prob = jax.nn.softmax(jnp.dot(xt, router_group, preferred_element_type=f32), axis=-1)
    g_gate, g_idx = lax.top_k(g_prob, 1)
    e_logits = jnp.dot(xt, router_expert, preferred_element_type=f32).reshape(T, N_GROUPS, EXPERTS_PER_GROUP)
    e_sel = e_logits[jnp.arange(T), g_idx[:, 0]]
    e_val, e_idx = lax.top_k(e_sel, TOP_K)
    gate = g_gate * jax.nn.softmax(e_val, axis=-1)
    expert = g_idx * EXPERTS_PER_GROUP + e_idx
    A = T * TOP_K
    e_flat = expert.reshape(A)
    w_flat = gate.reshape(A)
    tok_flat = jnp.repeat(jnp.arange(T, dtype=jnp.int32), TOP_K)
    order = jnp.argsort(e_flat)
    e_sorted = e_flat[order]
    counts = jnp.bincount(e_flat, length=N_EXPERTS)
    padded = (counts + MOE_BLOCK - 1) // MOE_BLOCK * MOE_BLOCK
    pad_end = jnp.cumsum(padded)
    pad_start = pad_end - padded
    start = jnp.cumsum(counts) - counts
    dest = pad_start[e_sorted] + (jnp.arange(A) - start[e_sorted])
    n_blocks = -(-(A + N_EXPERTS * (MOE_BLOCK - 1)) // MOE_BLOCK)
    P = n_blocks * MOE_BLOCK
    slot_tok = jnp.full((P,), T, dtype=jnp.int32).at[dest].set(tok_flat[order])
    slot_w = jnp.zeros((P,), f32).at[dest].set(w_flat[order])
    block_expert = jnp.minimum(jnp.searchsorted(pad_end, jnp.arange(n_blocks) * MOE_BLOCK, side='right'), N_EXPERTS - 1)
    x_pad = jnp.concatenate([xt, jnp.zeros((1, D), xt.dtype)], axis=0)

    def expert_block(args):
        toks, e = args
        xb = x_pad[toks]
        hb = jax.nn.silu(xb @ w_gate[e]) * (xb @ w_up[e])
        return hb @ w_down[e]

    y_blocks = lax.map(expert_block, (slot_tok.reshape(n_blocks, MOE_BLOCK), block_expert))
    y = jax.ops.segment_sum(y_blocks.reshape(P, D).astype(f32) * slot_w[:, None], slot_tok, num_segments=T + 1)[:T]
    return y.astype(h.dtype).reshape(B_, S, D)

def setup_inputs(seed: int = 0) -> dict:
    key = jax.random.key(seed)
    ks = jax.random.split(key, 24)

    def nrm(k, shape, scale):
        return jax.random.normal(k, shape, jnp.float32) * scale

    u = jax.random.uniform(ks[11], (N_EVEN, A_WIDTH), jnp.float32, minval=0.9, maxval=0.999)
    log_a = jnp.log(u) / RG_C
    rg_lambda = log_a - jnp.log(-jnp.expm1(log_a))
    return {
        "x": nrm(ks[0], (BATCH, SEQ, D_MODEL), 1.0),
        "norm_mix_g": 1.0 + nrm(ks[1], (DEPTH, D_MODEL), 0.02),
        "norm_ffn_g": 1.0 + nrm(ks[2], (DEPTH, D_MODEL), 0.02),
        "norm_final_g": 1.0 + nrm(ks[3], (D_MODEL,), 0.02),
        "ab_w_in": nrm(ks[4], (N_EVEN, D_MODEL, AB_IN), D_MODEL ** -0.5),
        "ab_conv_w": nrm(ks[5], (N_EVEN, CONV_WIDTH, A_WIDTH), CONV_WIDTH ** -0.5),
        "ab_conv_b": nrm(ks[6], (N_EVEN, A_WIDTH), 0.01),
        "rg_w_a": nrm(ks[7], (N_EVEN, A_BLOCKS, A_BLOCK, A_BLOCK), A_BLOCK ** -0.5),
        "rg_b_a": nrm(ks[8], (N_EVEN, A_WIDTH), 0.01),
        "rg_w_x": nrm(ks[9], (N_EVEN, A_BLOCKS, A_BLOCK, A_BLOCK), A_BLOCK ** -0.5),
        "rg_b_x": nrm(ks[10], (N_EVEN, A_WIDTH), 0.01),
        "rg_lambda": rg_lambda,
        "attn_rel_bias": nrm(ks[12], (N_EVEN, B_HEADS, 2 * REL_CLIP + 1), 0.1),
        "ab_w_out": nrm(ks[13], (N_EVEN, AB_MIX, D_MODEL), AB_MIX ** -0.5),
        "c_w_in": nrm(ks[14], (N_ODD, D_MODEL, C_IN), D_MODEL ** -0.5),
        "c_lb_logits": nrm(ks[15], (N_ODD + 1, C_WIDTH), 0.5),
        "c_norm_g": 1.0 + nrm(ks[16], (N_ODD, C_HEADS * C_DV), 0.02),
        "c_w_out": nrm(ks[17], (N_ODD, C_HEADS * C_DV, D_MODEL), (C_HEADS * C_DV) ** -0.5),
        "moe_router_group": nrm(ks[18], (DEPTH, D_MODEL, N_GROUPS), D_MODEL ** -0.5),
        "moe_router_expert": nrm(ks[19], (DEPTH, D_MODEL, N_EXPERTS), D_MODEL ** -0.5),
        "moe_w_gate": nrm(ks[20], (DEPTH, N_EXPERTS, D_MODEL, D_EXPERT), D_MODEL ** -0.5),
        "moe_w_up": nrm(ks[21], (DEPTH, N_EXPERTS, D_MODEL, D_EXPERT), D_MODEL ** -0.5),
        "moe_w_down": nrm(ks[22], (DEPTH, N_EXPERTS, D_EXPERT, D_MODEL), D_EXPERT ** -0.5),
    }

def reference(x, norm_mix_g, norm_ffn_g, norm_final_g, ab_w_in, ab_conv_w, ab_conv_b, rg_w_a, rg_b_a, rg_w_x, rg_b_x, rg_lambda, attn_rel_bias, ab_w_out, c_w_in, c_lb_logits, c_norm_g, c_w_out, moe_router_group, moe_router_expert, moe_w_gate, moe_w_up, moe_w_down):
    lb_all = jnp.cumsum(jax.nn.softmax(c_lb_logits.astype(jnp.float32), axis=0), axis=0)
    h = x
    for layer in range(DEPTH):
        j = layer // 2
        hn = rms_norm(h, norm_mix_g[layer])
        if layer % 2 == 0:
            mix = mixer_ab(hn, ab_w_in[j], ab_conv_w[j], ab_conv_b[j], rg_w_a[j], rg_b_a[j], rg_w_x[j], rg_b_x[j], rg_lambda[j], attn_rel_bias[j], ab_w_out[j])
        else:
            mix = hgrn2_mixer(hn, c_w_in[j], lb_all[j], c_norm_g[j], c_w_out[j])
        h = h + mix
        h = h + hier_moe(rms_norm(h, norm_ffn_g[layer]), moe_router_group[layer], moe_router_expert[layer], moe_w_gate[layer], moe_w_up[layer], moe_w_down[layer])
    return rms_norm(h, norm_final_g)


_drawn_inputs = setup_inputs


def setup_inputs(seed=0):
    import zlib

    import numpy as np

    out = dict(_drawn_inputs(seed))
    spreads = {}
    factors = {'norm_final_g': 8.991, 'rg_b_a': 22.563, 'rg_b_x': 5.039, 'c_norm_g': 3.296}
    for name, (base, spread) in spreads.items():
        noise = np.random.default_rng([zlib.crc32(name.encode()), seed]).standard_normal(out[name].shape)
        drawn = base * np.exp(spread * noise) if base else spread * noise
        out[name] = __import__('jax').numpy.asarray(drawn.astype(out[name].dtype))
    for name, factor in factors.items():
        out[name] = (out[name] * factor).astype(out[name].dtype)
    return out
```

```python
from contextlib import ExitStack

import numpy as np

import concourse.bass as bass
from concourse import mybir

ALU = mybir.AluOpType
ACT = mybir.ActivationFunctionType
AX = mybir.AxisListType
F32 = mybir.dt.float32
U32 = mybir.dt.uint32
I32 = mybir.dt.int32

P = 128
D = 1024
T = 512
NT = T // P
NC = D // P
EPS = 1e-6
HEADS_B = 8
AW = 512
CONV = 4
CLIP = 256
HEADS_C = 8
LEVELS = 7
NG, NPG = 4, 8
NE = NG * NPG
F = 512
FC = F // P
CAP = 64
BLOCKS = T // CAP
OFF = float(1 << 20)
GELU_A, GELU_B = 0.044715, 0.7978845608028654

COLS = [("mix_g", 2 * NC), ("ffn_g", 2 * NC), ("conv_w", 4 * CONV), ("conv_b", 4), ("b_a", 4), ("b_x", 4),
        ("lam", 4), ("lb0", 8), ("lb1", 8), ("norm_g", 8)]


class Banks:

    def __init__(self, count):
        self.uses = [0] * count
        self.jobs = {}

    def add(self, job, bank):
        self.jobs[job] = (bank, self.uses[bank])
        self.uses[bank] += 1


class Steps:

    def __init__(self, eng, sem):
        self.eng, self.sem, self.base, self.n = eng, sem, 0, 0

    def then(self, ins):
        self.n += 1
        ins.then_inc(self.sem, 1)
        self.eng.wait_ge(self.sem, self.base + self.n)


def trunk(nc, x, cols, final_g, ab_w_in, rg_w_a, rg_w_x, bias_rev, ab_w_out, c_w_in, c_w_out, router,
          w_gate, w_up, w_down, out, phases=4):
    with ExitStack() as ctx:
        def sb(name, shape, dt=F32):
            return ctx.enter_context(nc.sbuf_tensor("sb_" + name, shape, dt))

        def sem(name):
            return ctx.enter_context(nc.semaphore(name))

        h = sb("h", [P, NT, D])
        xh = sb("xh", [P, NT, D])
        xT = sb("xT", [P, NC, T])
        ident = sb("ident", [P, P])
        tri = sb("tri", [P, P])
        ones = sb("ones", [P, P])
        iota = sb("iota", [P, CAP])
        gkey = sb("gkey", [P, NG])
        ekey = sb("ekey", [P, NE])
        tokval = sb("tokval", [P, 2, NT])
        masks = sb("masks", [P, LEVELS, P])
        keep = sb("keep", [P, T])
        vec = sb("vec", [P, sum(n for _, n in COLS)])
        rt = sb("rt", [P, 2, NC, NG + NE])
        eps_t = sb("eps_t", [P, 1])
        ss = sb("ss", [P, 5, NT])
        std = sb("std", [P, 5, NT])
        rstd = sb("rstd", [P, 5, NT])
        ring_a = sb("ring_a", [P, 3, 8 * 512])
        ring_b = sb("ring_b", [P, 3, 8 * 512])
        xi = sb("xi", [CAP, NE], U32)
        ri = sb("ri", [CAP, NE], U32)
        gi = [sb(f"gi{j}", [CAP, 1], U32) for j in range(2)]
        si = [sb(f"si{j}", [CAP, 1], U32) for j in range(2)]
        xio = sb("xio", [CAP, BLOCKS * NE], U32)
        rio = sb("rio", [CAP, BLOCKS * NE], U32)
        flag = sb("flag", [P, 2], I32)
        gates = sb("gates", [P, 2, NT])
        lamt = sb("lamt", [P, 4, 4])
        cl = sb("cl", [P, 2, 4])
        lbt = sb("lbt", [P, 4, 8])
        lb = sb("lb", [P, 8])
        oml = sb("oml", [P, 8])
        scr = sb("scr", [P, 13000])
        xh_d = nc.dram_tensor("xh_rows", [2 * T, D], F32).ap()
        y_d = [nc.dram_tensor(f"expert_rows{l}", [2 * T, D], F32).ap() for l in range(2)]
        xg_d = [nc.dram_tensor(f"norm_rows{l}", [T, D], F32).ap() for l in range(2)]
        bias_d = nc.dram_tensor("bias_rows", [HEADS_B, 640], F32).ap()
        ps = [ctx.enter_context(nc.psum_tensor(f"ps{b}", [P, 512], F32)) for b in range(8)]

        at, o = {}, 0
        for name, n in COLS:
            at[name] = vec[:, o:o + n]
            o += n

        def flat(t):
            return t[:, :, :].rearrange("p a b -> p (a b)")

        def carve(base, sizes):
            views, pos = {}, 0
            for name, shape in sizes:
                n = int(np.prod(shape))
                v = base[:, pos:pos + n]
                if len(shape) == 2:
                    v = v.rearrange("p (a b) -> p a b", a=shape[0])
                elif len(shape) == 3:
                    v = v.rearrange("p (a b c) -> p a b c", a=shape[0], b=shape[1])
                views[name] = v
                pos += n
            assert pos <= base.shape[1], (pos, base.shape)
            return views

        m0 = carve(scr[:], [("y", (8, T)), ("q", (4, T)), ("k", (4, T)), ("strip", (2, T)), ("mx", (32,)),
                            ("nmx", (32,)), ("sum", (32,)), ("rs", (32,)), ("s", (3, T)), ("pt", (2, T)),
                            ("wa", (4, P)), ("wx", (4, P))])
        m0.update(carve(flat(ring_b), [("ga", (4, T)), ("xc", (4, T)), ("r", (4, T)), ("i", (4, T)), ("a", (4, T)),
                                       ("v", (4, T))]))
        m0.update(carve(flat(xh), [("xa", (4, T + 4))]))
        m0.update(carve(scr[:], [("rtab", (640,))]))
        m1 = carve(scr[:], [("q", (2, T)), ("kk", (2, T)), ("b", (2, T)), ("v", (2, T)), ("sg", (2, T)),
                            ("f", (T,)), ("e", (2, T)), ("qk", (2, T)), ("attn", (2, T)), ("eb", (T,)),
                            ("qe", (2, T)), ("dl", (3, P)), ("kh", (3, P)), ("st", (2, 3 * P)), ("sq", (T,)),
                            ("rs", (T,))])
        m1.update(carve(flat(xh), [("y", (8, T))]))
        me = carve(scr[:], [("rows", (4, D)), ("xgT", (2, NC * CAP)), ("hT", (2, FC * CAP)), ("silu", (2, FC * CAP)),
                            ("yT", (2, NC * CAP)), ("lg", (NT, NG + NE)), ("em", (NT, NE)), ("key", (NT, NE)),
                            ("M0", (NT, NE)), ("M1", (NT, NE)), ("M", (NT, NE)), ("pos", (2, NT)),
                            ("A", (2, NT, CAP)), ("B", (2, NT, NE)), ("g4", (NT, NG)), ("goh", (NT, NG)),
                            ("ex", (NT, 5)), ("tab", (3, NE)), ("w", (12, NT)), ("fin_g", (D,))])

        filled = [sem(f"filled{b}") for b in range(8)]
        drained = [sem(f"drained{b}") for b in range(8)]
        ring_in = {(r, s): sem(f"ring_in_{r}{s}") for r in "ab" for s in range(3)}
        x_in, vec_in, diag_in, router_in, final_in = (sem(n) for n in ("x_in", "vec_in", "diag_in", "router_in",
                                                                       "final_in"))
        rtab_in, rtab_full, rtab_out, strip_ready = (sem(n) for n in ("rtab_in", "rtab_full", "rtab_out",
                                                                      "strip_ready"))
        strip_in = [sem(f"strip_in{j}") for j in range(2)]
        made, dve_made, diag_zero, eps_made = (sem(n) for n in ("made", "dve_made", "diag_zero", "eps_made"))
        dve_step, pool_step = sem("dve_step"), sem("pool_step")
        lam_exp, cl_ready, lb_in, lb_exp, lb_ready = (sem(n) for n in ("lam_exp", "cl_ready", "lb_in", "lb_exp",
                                                                       "lb_ready"))
        lam_in = sem("lam_in")
        ss_ready, std_ready, rstd_ready, xh_ready, h_ready = (sem(n) for n in ("ss_ready", "std_ready", "rstd_ready",
                                                                               "xh_ready", "h_ready"))
        out_ready, out_stored = sem("out_ready"), sem("out_stored")
        xc_ready, rg_x, rg_a, rg_t, rg_m2, rg_m, gelu_in, gelu_t, ya_ready = (
            sem(n) for n in ("xc_ready", "rg_x", "rg_a", "rg_t", "rg_m2", "rg_m", "gelu_in", "gelu_t", "ya_ready"))
        score_max, prob_exp, prob_ready = sem("score_max"), sem("prob_exp"), sem("prob_ready")
        (f_ready, kk_ready, lf_ready, b_ready, sgg_ready, e_sub, e_exp, qk_ready, eb_ready, dl_sub, dl_exp, qe_ready,
         kh_ready, osq_ready, rs_ready, y_ready) = (
            sem(n) for n in ("f_ready", "kk_ready", "lf_ready", "b_ready", "sgg_ready", "e_sub", "e_exp", "qk_ready",
                             "eb_ready", "dl_sub", "dl_exp", "qe_ready", "kh_ready", "osq_ready", "rs_ready",
                             "y_ready"))
        (xh_stored, route_in, route_exp, one_hot, slots_hot, table_ready, flag_ready, ring_done) = (
            sem(n) for n in ("xh_stored", "route_in", "route_exp", "one_hot", "slots_hot", "table_ready",
                             "flag_ready", "ring_done"))
        pool_rows = sem("pool_rows")
        ov_done = sem("more_done")
        moving = sem("moving")
        turning = sem("turning")
        hidden = sem("hidden")
        idx_copied = sem("idx_copied")
        gathered = [sem(f"gathered{j}") for j in range(2)]
        scattered = [sem(f"scattered{j}") for j in range(2)]
        yrow_in = [sem(f"yrow_in{j}") for j in range(2)]
        ov = [{k: sem(f"more{l}_{k}") for k in ("w", "pe", "dve", "act", "idx", "gather", "scatter", "tab", "tabpe",
                                                "step")} for l in range(2)]

        bk = Banks(8)
        moe_base = []
        NA = HEADS_B * NT

        def plan_norm(n):
            for t in range(NT):
                for half in range(2):
                    bk.add(("xt", n, t, half), 2 * t + half)

        def plan_out(l):
            for nb in range(2):
                for t in range(NT):
                    bk.add(("out", l, t, nb), nb * 4 + t)

        def plan_moe(l):
            bk.add(("lg", l), 6)
            bk.add(("pos", l), 7)
            bk.add(("tab", l), 6)
            moe_base.append(list(bk.uses))
            for b in range(6):
                bk.uses[b] += NE

        plan_norm(0)
        for name, first in (("xa", 0), ("ga", 4), ("q", 0)):
            for m in range(4):
                bk.add((name, m), first + m)
        for m in range(4):
            bk.add(("ra", m), 4 + m % 2)
            bk.add(("ix", m), 6 + m % 2)
        for name, first in (("k", 0), ("v", 4)):
            for m in range(4):
                bk.add((name, m), first + m)
        for n in range(NA + 2):
            if n < NA:
                bk.add(("S", n), n % 2)
            if 1 <= n <= NA:
                bk.add(("T", n - 1), 2 + (n - 1) % 2)
            if n >= 2:
                bk.add(("O", n - 2), 4 + n % 2)
        plan_out(0)
        plan_norm(1)
        plan_moe(0)
        plan_norm(2)
        for H in range(HEADS_C + 2):
            for k in range(4):
                if H < HEADS_C:
                    bk.add(("c", H, k), k)
                if k == 0 and H >= 2:
                    bk.add(("o", H - 2), 7)
                if k == 1 and H >= 2:
                    bk.add(("osum", H - 2), 6)
                if 1 <= H <= HEADS_C:
                    for L in (2 * k, 2 * k + 1):
                        bk.add(("lev", H - 1, L), 4 + L % 2)
                    if k == 1:
                        bk.add(("khT", H - 1), 6)
                    if k == 2:
                        bk.add(("dst", H - 1), 6)
        plan_out(1)
        plan_norm(3)
        plan_moe(1)

        def wait_full(eng, job):
            b, n = bk.jobs[job]
            eng.wait_ge(filled[b], n + 1)

        def wait_drained(eng, job):
            b, n = bk.jobs[job]
            eng.wait_ge(drained[b], n + 1)

        def drains(ins, job):
            ins.then_inc(drained[bk.jobs[job][0]], 1)

        def bank(job):
            return ps[bk.jobs[job][0]]

        BX, BG, BU, BY, BZ = 0, 1, 2, 3, 4
        rings = {"a": ring_a, "b": ring_b}

        loads = {key: 0 for key in ring_in}
        w0_in, w1_in, e_loads = [], [], []

        def place(lst, r, s):
            loads[(r, s)] += 1
            lst.append((r, s, loads[(r, s)]))

        for i in range(7):
            place(w0_in, "a", i % 3)
        for l in range(2):
            if l == 1:
                for i in range(HEADS_C):
                    place(w1_in, "a", i % 3)
                place(w1_in, "a", 2)
                place(w1_in, "a", 0)
            e_loads.append(dict(loads))
            for key in loads:
                loads[key] += NE // 2

        def wblock(r, s, n):
            return rings[r][:, s, :].rearrange("p (c n) -> p c n", c=n)

        def exp_ring(j):
            return "ba"[j]

        block = ctx.enter_context(nc.Block())

        @block.sync
        def _(sp):
            for t in range(NT):
                sp.dma_start(h[:, t, :], x[0, t * P:(t + 1) * P, :]).then_inc(x_in, 16)
            sp.dma_start(vec[:], cols).then_inc(vec_in, 16)

            def w0_load(i):
                r, s, _ = w0_in[i]
                src = ab_w_in[0][:, i * 512:(i + 1) * 512] if i < 5 else \
                    ab_w_out[0][:, (i - 5) * 512:(i - 4) * 512]
                sp.dma_start(wblock(r, s, NC), src.rearrange("(c p) n -> p c n", p=P)).then_inc(ring_in[(r, s)], 16)

            w0_load(0)
            w0_load(1)
            sp.wait_ge(diag_zero, 2)
            for dst, src in ((m0["wa"], rg_w_a), (m0["wx"], rg_w_x)):
                for par in range(2):
                    sp.dma_start(dst[64 * par:64 * par + 64, :, 64 * par:64 * par + 64],
                                 src[0, par::2].rearrange("n c d -> c n d")).then_inc(diag_in, 16)
            w0_load(2)
            sp.dma_start(m0["rtab"][0:HEADS_B, 255:639], bias_rev[:, 0:384]).then_inc(rtab_in, 16)
            sp.wait_ge(rtab_full, 2)
            sp.dma_start(bias_d, m0["rtab"][0:HEADS_B, :]).then_inc(rtab_out, 16)
            sp.wait_ge(rtab_out, 16)

            def strip(hd):
                if hd >= 2:
                    wait_drained(sp, ("S", 4 * (hd - 2) + 3))
                sp.dma_start(m0["strip"][:, hd % 2, :],
                             bass.AP(tensor=bias_d.tensor, offset=hd * 640, ap=[[1, P], [1, T]])
                             ).then_inc(strip_in[hd % 2], 16)

            strip(0)
            strip(1)
            sp.dma_start(rt[:].rearrange("p a b c -> p (a b c)"), router).then_inc(router_in, 16)
            last_of = [("xa", 3), ("ga", 3), ("q", 3), ("k", 3), ("v", 3)]
            for i in range(3, 7):
                wait_full(sp, last_of[i - 3])
                w0_load(i)
            for hd in range(2, HEADS_B):
                strip(hd)

            def expert_load(l, e, j, first):
                r = exp_ring(j)
                srcs = [w[l, bass.ds(e, 1)].rearrange("a (c p) n -> p (a c) n", p=P) for w in (w_gate, w_up, w_down)]
                for s, b in enumerate((BG, BU, BY)):
                    if not first:
                        sp.wait_ge(filled[b], e + (moe_base[l][b] - 1))
                    sp.dma_start(wblock(r, s, (NC, NC, FC)[s]), srcs[s]).then_inc(ring_in[(r, s)], 16)

            def moe_loads(l):
                if l == 0:
                    sp.wait_ge(ya_ready, 1)
                    wait_full(sp, ("O", NA - 1))
                expert_load(l, 0, 0, True)
                for nb in range(2):
                    wait_full(sp, ("out", l, NT - 1, nb))
                expert_load(l, 1, 1, True)
                with sp.Fori(0, NE // 2 - 1) as i:
                    expert_load(l, i * 2 + 2, 0, False)
                    expert_load(l, i * 2 + 3, 1, False)

            def more_loads(l):
                sp.wait_ge(flag_ready, l + 1)
                more = sp.value_load(flag[0:1, l:l + 1], min_val=0, max_val=1)
                o = ov[l]
                with sp.If(more > 0):
                    with sp.Fori(0, NE) as e:
                        srcs = [w[l, bass.ds(e, 1)].rearrange("a (c p) n -> p (a c) n", p=P)
                                for w in (w_gate, w_up, w_down)]
                        sp.wait_ge(o["pe"], e * (5 * (BLOCKS - 1)) + 1)
                        for s in range(3):
                            sp.dma_start(wblock("a", s, (NC, NC, FC)[s]), srcs[s]).then_inc(o["w"], 16)

            moe_loads(0)
            more_loads(0)
            sp.wait_ge(ring_done, 1)
            for i, (r, s, _) in enumerate(w1_in):
                if 3 <= i < HEADS_C:
                    wait_full(sp, ("c", i - 3, 3))
                if i >= HEADS_C:
                    wait_full(sp, ("c", i - 3, 3))
                if i < HEADS_C:
                    sp.dma_start(rings[r][:, s, :], c_w_in[i]).then_inc(ring_in[(r, s)], 16)
                else:
                    nb = i - HEADS_C
                    sp.dma_start(wblock(r, s, NC), c_w_out[0][:, nb * 512:(nb + 1) * 512]
                                 .rearrange("(c p) n -> p c n", p=P)).then_inc(ring_in[(r, s)], 16)
            moe_loads(1)
            more_loads(1)
            for t in range(NT):
                sp.wait_ge(out_ready, t + 1)
                sp.dma_start(out[0, t * P:(t + 1) * P, :], xh[:, t, :]).then_inc(out_stored, 16)
            sp.wait_ge(out_stored, 16 * NT)

        @block.tensor
        def _(pe):
            def opens(job):
                b, n = bk.jobs[job]
                if n > 0:
                    pe.wait_ge(drained[b], n)
                return ps[b]

            def fills(ins, job):
                ins.then_inc(filled[bk.jobs[job][0]], 1)

            def turn_rows(n):
                for t in range(NT):
                    pe.wait_ge(xh_ready, n * NT + t + 1)
                    for half in range(2):
                        job = ("xt", n, t, half)
                        dst = opens(job)
                        for c in range(4):
                            mm = nc.tensor.transpose(dst[:, c * P:(c + 1) * P],
                                                     xh[:, t, (half * 4 + c) * P:(half * 4 + c + 1) * P], ident[:])
                        fills(mm, job)

            def xT_ready(n, tiles=range(NT)):
                for t in tiles:
                    for half in range(2):
                        wait_drained(pe, ("xt", n, t, half))

            def out_proj(l, blocks, y):
                for nb, (r, s, k) in enumerate(blocks):
                    pe.wait_ge(ring_in[(r, s)], 16 * k)
                    w = wblock(r, s, NC)
                    for t in range(NT):
                        job = ("out", l, t, nb)
                        dst = opens(job)
                        for c in range(NC):
                            mm = nc.tensor.matmul(dst[:], y[:, c, t * P:(t + 1) * P], w[:, c, :],
                                                  start=(c == 0), stop=(c == NC - 1))
                        fills(mm, job)

            def proj0(i, name):
                r, s, k = w0_in[i]
                pe.wait_ge(ring_in[(r, s)], 16 * k)
                w = wblock(r, s, NC)
                for m in range(4):
                    job = (name, m)
                    dst = opens(job)
                    for c in range(NC):
                        if name == "v":
                            a, b = xT[:, c, m * P:(m + 1) * P], w[:, c, :]
                        else:
                            a, b = w[:, c, m * P:(m + 1) * P], xT[:, c, :]
                        mm = nc.tensor.matmul(dst[:], a, b, start=(c == 0), stop=(c == NC - 1))
                    fills(mm, job)

            def scores(n):
                hd, i = n // NT, n % NT
                if n == 0:
                    for m in range(4):
                        wait_drained(pe, ("q", m))
                        wait_drained(pe, ("k", m))
                lo = 64 * (hd % 2)
                dst = opens(("S", n))
                fills(nc.tensor.matmul(dst[:, 0:(i + 1) * P], m0["q"][lo:lo + 64, hd // 2, i * P:(i + 1) * P],
                                       m0["k"][lo:lo + 64, hd // 2, 0:(i + 1) * P], start=True, stop=True), ("S", n))

            def turn_probs(n):
                i = n % NT
                pe.wait_ge(prob_ready, n + 1)
                dst = opens(("T", n))
                for kt in range(i + 1):
                    mm = nc.tensor.transpose(dst[:, kt * P:(kt + 1) * P], m0["s"][:, n % 3, kt * P:(kt + 1) * P],
                                             ident[:])
                fills(mm, ("T", n))

            def values(n):
                hd, i = n // NT, n % NT
                if n == 0:
                    for m in range(4):
                        wait_drained(pe, ("v", m))
                wait_drained(pe, ("T", n))
                lo = 64 * (hd % 2)
                dst = opens(("O", n))
                for kt in range(i + 1):
                    mm = nc.tensor.matmul(dst[lo:lo + 64, 0:P], m0["v"][:, kt, hd * 64:(hd + 1) * 64],
                                          m0["pt"][:, n % 2, kt * P:(kt + 1) * P], start=(kt == 0), stop=(kt == i))
                fills(mm, ("O", n))

            pe.wait_ge(made, 1)
            turn_rows(0)
            xT_ready(0)
            proj0(0, "xa")
            proj0(1, "ga")
            proj0(2, "q")
            pe.wait_ge(diag_in, 64)
            for m in range(4):
                pe.wait_ge(xc_ready, m + 1)
                for name, w in (("ra", m0["wa"]), ("ix", m0["wx"])):
                    dst = opens((name, m))
                    fills(nc.tensor.matmul(dst[:], w[:, m, :], m0["xc"][:, m, :], start=True, stop=True), (name, m))
            proj0(3, "k")
            proj0(4, "v")
            for n in range(NA + 2):
                if n < NA:
                    scores(n)
                if 1 <= n <= NA:
                    turn_probs(n - 1)
                if n >= 2:
                    values(n - 2)
            pe.wait_ge(ya_ready, 1)
            for n in (NA - 2, NA - 1):
                wait_drained(pe, ("O", n))
            out_proj(0, w0_in[5:7], m0["y"])

            def rows_in(l, e, k, j):
                pe.wait_ge(gathered[j], k * 16 + 16 * (l * (NE // 2) + 1))
                pe.wait_ge(drained[BX], e + moe_base[l][BX])
                pe.sem_inc(turning, 1)
                for c in range(NC):
                    mm = nc.tensor.transpose(ps[BX][:, c * CAP:(c + 1) * CAP],
                                             me["rows"][0:CAP, j, c * P:(c + 1) * P], ident[0:CAP, 0:CAP])
                mm.then_inc(filled[BX], 1)

            def widen(b, w, src):
                out_c, in_c = w.shape[2] // P, w.shape[1]
                for m in range(out_c):
                    for c in range(in_c):
                        mm = nc.tensor.matmul(ps[b][:, m * CAP:(m + 1) * CAP], w[:, c, m * P:(m + 1) * P],
                                              src[:, c * CAP:(c + 1) * CAP], start=(c == 0), stop=(c == in_c - 1))
                return mm

            def rows_back(src):
                for z in range(2):
                    for c in range(4):
                        mm = nc.tensor.transpose(ps[BZ + z][0:CAP, c * P:(c + 1) * P],
                                                 src[:, (z * 4 + c) * CAP:(z * 4 + c + 1) * CAP], ident[:])
                    yield z, mm

            def rows_out(l, e, j):
                pe.wait_ge(drained[BY], e + (moe_base[l][BY] + 1))
                for z in range(2):
                    pe.wait_ge(drained[BZ + z], e + moe_base[l][BZ + z])
                pe.sem_inc(turning, 1)
                for z, mm in rows_back(me["yT"][:, j, :]):
                    mm.then_inc(filled[BZ + z], 1)

            def expert(l, e, k, j, first=False, last=False):
                base, r = moe_base[l], exp_ring(j)
                pe.wait_ge(drained[BX], e + (base[BX] + 1))
                for s, b in ((0, BG), (1, BU)):
                    pe.wait_ge(ring_in[(r, s)], k * 16 + 16 * (e_loads[l][(r, s)] + 1))
                    pe.wait_ge(drained[b], e + base[b])
                    widen(b, wblock(r, s, NC), me["xgT"][:, j, :]).then_inc(filled[b], 1)
                if not last:
                    rows_in(l, e + 1, k + j, 1 - j)
                if not first:
                    rows_out(l, e - 1, 1 - j)
                pe.wait_ge(ring_in[(r, 2)], k * 16 + 16 * (e_loads[l][(r, 2)] + 1))
                pe.wait_ge(hidden, e + (l * NE + 1))
                pe.wait_ge(drained[BY], e + base[BY])
                widen(BY, wblock(r, 2, FC), me["hT"][:, j, :]).then_inc(filled[BY], 1)

            def more_blocks(l):
                pe.wait_ge(flag_ready, l + 1)
                more = pe.value_load(flag[0:1, l:l + 1], min_val=0, max_val=1)
                o, per_e = ov[l], BLOCKS - 1
                with pe.If(more > 0):
                    for z in range(2):
                        pe.wait_ge(drained[BZ + z], moe_base[l][BZ + z] + NE)
                    pe.sem_inc(o["pe"], 1)
                    with pe.Fori(0, per_e) as b:
                        pe.wait_ge(o["tab"], b * 2 + 1)
                        for i in range(2 * NT):
                            mm = nc.tensor.matmul(ps[6][0:CAP, 0:NE], me["A"][:, i // NT, i % NT, :],
                                                  me["B"][:, i // NT, i % NT, :], start=(i == 0), stop=(i == 2 * NT - 1))
                        mm.then_inc(o["tabpe"], 1)
                    with pe.Fori(0, NE) as e:
                        with pe.Fori(0, per_e) as b:
                            n = e * per_e + b
                            pe.wait_ge(o["w"], e * 48 + 48)
                            pe.wait_ge(o["gather"], n * 16 + 16)
                            pe.sem_inc(turning, 1)
                            for c in range(NC):
                                mm = nc.tensor.transpose(ps[BX][:, c * CAP:(c + 1) * CAP],
                                                         me["rows"][0:CAP, 0, c * P:(c + 1) * P], ident[0:CAP, 0:CAP])
                            mm.then_inc(o["pe"], 1)
                            pe.wait_ge(o["dve"], n * 4 + 1)
                            for s, bb in ((0, BG), (1, BU)):
                                widen(bb, wblock("a", s, NC), me["xgT"][:, 0, :]).then_inc(o["pe"], 1)
                            pe.wait_ge(o["dve"], n * 4 + 2)
                            widen(BY, wblock("a", 2, FC), me["hT"][:, 0, :]).then_inc(o["pe"], 1)
                            pe.wait_ge(o["act"], n * 2 + 2)
                            pe.sem_inc(turning, 1)
                            for z, mm in rows_back(me["yT"][:, 0, :]):
                                pass
                            mm.then_inc(o["pe"], 1)

            def moe(l):
                n = 2 * l + 1
                turn_rows(n)
                pe.wait_ge(router_in, 16)
                dst = opens(("lg", l))
                for t in range(NT):
                    xT_ready(n, [t])
                    for c in range(NC):
                        mm = nc.tensor.matmul(dst[:, t * 64:t * 64 + NG + NE], xT[:, c, t * P:(t + 1) * P],
                                              rt[:, l, c, :], start=(c == 0), stop=(c == NC - 1))
                fills(mm, ("lg", l))
                pe.wait_ge(one_hot, l + 1)
                dst = opens(("pos", l))
                for t in range(NT):
                    for u in range(t + 1):
                        nc.tensor.matmul(dst[:, t * NE:(t + 1) * NE], (tri if u == t else ones)[:], me["M"][:, u, :],
                                         start=(u == 0), stop=(u == t))
                for u in range(NT):
                    mm = nc.tensor.matmul(dst[:, 256:256 + NE], ones[:], me["M"][:, u, :],
                                          start=(u == 0), stop=(u == NT - 1))
                fills(mm, ("pos", l))
                pe.wait_ge(slots_hot, l + 1)
                dst = opens(("tab", l))
                for i in range(2 * NT):
                    mm = nc.tensor.matmul(dst[0:CAP, 0:NE], me["A"][:, i // NT, i % NT, :],
                                          me["B"][:, i // NT, i % NT, :], start=(i == 0), stop=(i == 2 * NT - 1))
                fills(mm, ("tab", l))
                rows_in(l, 0, 0, 0)
                expert(l, 0, 0, 0, first=True)
                with pe.Fori(0, NE // 2 - 1) as i:
                    expert(l, i * 2 + 1, i, 1)
                    expert(l, i * 2 + 2, i + 1, 0)
                expert(l, NE - 1, NE // 2 - 1, 1, last=True)
                rows_out(l, NE - 1, 1)
                more_blocks(l)

            moe(0)
            pe.sem_inc(ring_done, 1)

            def proj1(H, k):
                r, s, n = w1_in[H]
                if k == 0:
                    pe.wait_ge(ring_in[(r, s)], 16 * n)
                w = rings[r][:, s, :].rearrange("p (c k n) -> p c k n", c=NC, k=4)
                dst = opens(("c", H, k))
                if k == 2:
                    for t in range(NT):
                        for c in range(NC):
                            mm = nc.tensor.matmul(dst[:, t * P:(t + 1) * P], xT[:, c, t * P:(t + 1) * P], w[:, c, k, :],
                                                  start=(c == 0), stop=(c == NC - 1))
                else:
                    for c in range(NC):
                        mm = nc.tensor.matmul(dst[:], w[:, c, k, :], xT[:, c, :], start=(c == 0), stop=(c == NC - 1))
                fills(mm, ("c", H, k))

            def level(H, L):
                if L == 0:
                    wait_drained(pe, ("c", H, 1))
                    pe.wait_ge(kk_ready, H + 1)
                    a, b = m1["kk"][:, H % 2, :], m1["q"][:, H % 2, :]
                else:
                    pe.wait_ge(qk_ready, H * LEVELS + L)
                    a = b = m1["qk"][:, L % 2, :]
                dst = opens(("lev", H, L))
                for j in range(NT):
                    sl = slice(j * P, (j + 1) * P)
                    mm = nc.tensor.matmul(dst[:, sl], a[:, sl], b[:, sl], start=True, stop=True)
                fills(mm, ("lev", H, L))

            def turn_keys(H):
                pe.wait_ge(kh_ready, H + 1)
                dst = opens(("khT", H))
                for j in range(NT - 1):
                    mm = nc.tensor.transpose(dst[:, j * P:(j + 1) * P], m1["dl"][:, j, :], ident[:])
                fills(mm, ("khT", H))

            def chunk_states(H):
                wait_drained(pe, ("khT", H))
                wait_drained(pe, ("c", H, 2))
                dst = opens(("dst", H))
                for j in range(NT - 1):
                    sl = slice(j * P, (j + 1) * P)
                    mm = nc.tensor.matmul(dst[:, sl], m1["kh"][:, j, :], m1["v"][:, H % 2, sl], start=True, stop=True)
                fills(mm, ("dst", H))

            def head_out(H):
                wait_drained(pe, ("lev", H, LEVELS))
                wait_drained(pe, ("dst", H))
                pe.wait_ge(qe_ready, H + 1)
                dst = opens(("o", H))
                for j in range(NT):
                    sl = slice(j * P, (j + 1) * P)
                    mm = nc.tensor.matmul(dst[:, sl], m1["v"][:, H % 2, sl], m1["attn"][:, H % 2, sl],
                                          start=True, stop=(j == 0))
                    if j > 0:
                        mm = nc.tensor.matmul(dst[:, sl], m1["st"][:, H % 2, (j - 1) * P:j * P], m1["qe"][:, H % 2, sl],
                                              start=False, stop=True)
                fills(mm, ("o", H))

            def head_sum(H):
                pe.wait_ge(osq_ready, H + 1)
                dst = opens(("osum", H))
                fills(nc.tensor.matmul(dst[:], ones[:], m1["sq"][:], start=True, stop=True), ("osum", H))

            turn_rows(2)
            xT_ready(2)
            for H in range(HEADS_C + 2):
                for k in range(4):
                    if H < HEADS_C:
                        proj1(H, k)
                    if k == 0 and H >= 2:
                        head_out(H - 2)
                    if k == 1 and H >= 2:
                        head_sum(H - 2)
                    if 1 <= H <= HEADS_C:
                        level(H - 1, 2 * k)
                        level(H - 1, 2 * k + 1)
                        if k == 1:
                            turn_keys(H - 1)
                        if k == 2:
                            chunk_states(H - 1)
            pe.wait_ge(y_ready, HEADS_C)
            out_proj(1, w1_in[8:10], m1["y"])
            moe(1)

        @block.scalar
        def _(act):
            A = nc.scalar.activation

            def norm(n):
                for t in range(NT):
                    if n == 0:
                        act.wait_ge(x_in, 16 * NT)
                    elif n % 2 == 1:
                        for nb in range(2):
                            wait_drained(act, ("out", n // 2, t, nb))
                    else:
                        act.wait_ge(h_ready, (n // 2 - 1) * 2 * NT + 2 * t + 2)
                    if n == 0 and t == 0:
                        act.wait_ge(eps_made, 1)
                    if n == 3 and t == 0:
                        wait_full(act, ("out", 1, NT - 1, 1))
                    A(xh[:, t, :], h[:, t, :], ACT.Square, accum_out=ss[:, n, t:t + 1]).then_inc(ss_ready, 1)
                    act.wait_ge(ss_ready, n * NT + t + 1)
                    A(std[:, n, t:t + 1], ss[:, n, t:t + 1], ACT.Sqrt, bias=eps_t[:, 0:1], scale=1.0 / D
                      ).then_inc(std_ready, 1)
                    act.wait_ge(rstd_ready, n * NT + t + 1)
                    A(xh[:, t, :], h[:, t, :], ACT.Copy, scale=rstd[:, n, t:t + 1]).then_inc(xh_ready, 1)
                    if n % 2 == 1:
                        l = n // 2
                        act.wait_ge(xh_ready, n * NT + t + 1)
                        act.dma_start(xg_d[l][t * P:(t + 1) * P, :], xh[:, t, :]).then_inc(xh_stored, 16)

            norm(0)
            act.wait_ge(lam_in, 1)
            A(lamt[:, 1, :], lamt[:, 0, :], ACT.Exp, scale=-1.0).then_inc(lam_exp, 1)
            act.wait_ge(lb_in, 2)
            A(lbt[:, 2:4, :], lbt[:, 0:2, :], ACT.Exp).then_inc(lb_exp, 1)

            for m in range(4):
                wait_full(act, ("xa", m))
                drains(A(m0["xa"][:, m, 3:3 + T], bank(("xa", m))[:], ACT.Copy), ("xa", m))
            for m in range(4):
                wait_full(act, ("ga", m))
                drains(A(m0["ga"][:, m, :], bank(("ga", m))[:], ACT.Copy), ("ga", m))
            for m in range(4):
                for name, dst, b in (("ra", "r", "b_a"), ("ix", "i", "b_x")):
                    wait_full(act, (name, m))
                    drains(A(m0[dst][:, m, :], bank((name, m))[:], ACT.Sigmoid, bias=at[b][:, m:m + 1]), (name, m))
            act.wait_ge(cl_ready, 2)
            for m in range(4):
                wait_drained(act, ("ra", m))
                A(m0["a"][:, m, :], m0["r"][:, m, :], ACT.Exp, scale=cl[:, 0, m:m + 1]).then_inc(rg_a, 1)
            act.wait_ge(rg_a, 4)
            for m in range(4):
                A(m0["r"][:, m, :], m0["r"][:, m, :], ACT.Tanh, scale=cl[:, 1, m:m + 1]).then_inc(rg_t, 1)
            act.wait_ge(gelu_in, 1)
            A(m0["xa"][:, :, 0:T], m0["xa"][:, :, 0:T], ACT.Tanh, scale=GELU_B).then_inc(gelu_t, 1)
            for m in range(4):
                wait_full(act, ("k", m))
                drains(A(m0["k"][:, m, :], bank(("k", m))[:], ACT.Copy), ("k", m))
            act.wait_ge(rg_m2, 1)
            A(m0["xc"], m0["xc"], ACT.Sqrt).then_inc(rg_m, 1)
            for m in range(4):
                wait_full(act, ("v", m))
                drains(A(m0["v"][:, m, :], bank(("v", m))[:], ACT.Copy), ("v", m))
            for n in range(NA + 1):
                if n < NA:
                    N = (n % NT + 1) * P
                    act.wait_ge(score_max, n + 1)
                    A(m0["s"][:, n % 3, 0:N], m0["s"][:, n % 3, 0:N], ACT.Exp, bias=m0["nmx"][:, n:n + 1],
                      accum_out=m0["sum"][:, n:n + 1]).then_inc(prob_exp, 1)
                if n >= 1:
                    q = n - 1
                    N = (q % NT + 1) * P
                    wait_full(act, ("T", q))
                    if q >= 2:
                        wait_full(act, ("O", q - 2))
                    drains(A(m0["pt"][:, q % 2, 0:N], bank(("T", q))[:, 0:N], ACT.Copy), ("T", q))

            def act_expert(l, e, j, jz, first=False, idle=False):
                base = moe_base[l]
                act.wait_ge(filled[BG], e + (base[BG] + 1))
                if not first:
                    act.wait_ge(hidden, e + (l * NE - (1 if l or not isinstance(e, int) or e > 1 else 0)))
                A(me["silu"][:, j, :], ps[BG][:, 0:FC * CAP], ACT.Silu).then_inc(drained[BG], 1)
                if not first:
                    half_rows(l, e - 1, jz)
                act.wait_ge(filled[BY], e + (base[BY] + 1))
                if not first:
                    act.wait_ge(filled[BZ + 1], e + (base[BZ + 1]))
                A(me["yT"][:, j, :], ps[BY][:], ACT.Copy).then_inc(drained[BY], 1)

            def half_rows(l, e, j):
                base = moe_base[l]
                act.wait_ge(filled[BZ + 1], e + (base[BZ + 1] + 1))
                A(me["rows"][0:CAP, 2 + j, 512:1024], ps[BZ + 1][0:CAP, :], ACT.Copy).then_inc(drained[BZ + 1], 1)

            def more_blocks(l):
                act.wait_ge(flag_ready, l + 1)
                more = act.value_load(flag[0:1, l:l + 1], min_val=0, max_val=1)
                o = ov[l]
                with act.If(more > 0):
                    with act.Fori(0, NE * (BLOCKS - 1)) as n:
                        act.wait_ge(o["pe"], n * 5 + 3)
                        A(me["silu"][:, 0, :], ps[BG][:, 0:FC * CAP], ACT.Silu).then_inc(o["act"], 1)
                        act.wait_ge(o["pe"], n * 5 + 5)
                        A(me["yT"][:, 0, :], ps[BY][:], ACT.Copy).then_inc(o["act"], 1)

            def moe(l):
                norm(2 * l + 1)
                act.wait_ge(route_in, l + 1)
                A(me["ex"], me["ex"], ACT.Exp).then_inc(route_exp, 1)
                SCATTER_BASE = l * (NE // 2)
                act_expert(l, 0, 0, 0, first=True)
                act_expert(l, 1, 1, 0)
                with act.Fori(0, NE // 2 - 1) as i:
                    act.wait_ge(scattered[1], i * 16 + 16 * SCATTER_BASE) if False else None
                    act_expert(l, i * 2 + 2, 0, 1)
                    act.wait_ge(scattered[0], i * 16 + 16 * (SCATTER_BASE + 1))
                    act_expert(l, i * 2 + 3, 1, 0)
                act.wait_ge(scattered[1], 16 * (SCATTER_BASE + NE // 2 - 1))
                half_rows(l, NE - 1, 1)
                more_blocks(l)
                for j in range(2):
                    act.wait_ge(scattered[j], 16 * (SCATTER_BASE + NE // 2))
                act.wait_ge(ov_done, l + 1)
                for t in range(NT):
                    if t >= 2:
                        act.wait_ge(h_ready, l * 2 * NT + 2 * (t - 1))
                    for k in range(2):
                        act.dma_start(me["rows"][:, 2 * (t % 2) + k, :],
                                      y_d[l][k * T + t * P:k * T + (t + 1) * P, :]).then_inc(yrow_in[t % 2], 16)

            moe(0)
            norm(2)

            def exp_level(G, L):
                act.wait_ge(e_sub, G * LEVELS + L)
                A(m1["e"][:, L % 2, :], m1["e"][:, L % 2, :], ACT.Exp).then_inc(e_exp, 1)

            for H in range(HEADS_C + 2):
                new, G, O = H < HEADS_C, H - 1, H - 2
                core, outp = 0 <= G < HEADS_C, O >= 0
                if core:
                    exp_level(G, 1)
                    exp_level(G, 2)
                    act.wait_ge(b_ready, G + 1)
                    if G > 0:
                        act.wait_ge(qe_ready, G)
                        wait_drained(act, ("dst", G - 1))
                    A(m1["eb"], m1["b"][:, G % 2, :], ACT.Exp).then_inc(eb_ready, 1)
                    act.wait_ge(dl_sub, G + 1)
                    A(m1["dl"], m1["dl"], ACT.Exp).then_inc(dl_exp, 1)
                if new:
                    wait_full(act, ("c", H, 0))
                    if H > 0:
                        act.wait_ge(kk_ready, H)
                        act.wait_ge(lf_ready, H)
                    drains(A(m1["f"], bank(("c", H, 0))[:], ACT.Sigmoid), ("c", H, 0))
                if outp:
                    wait_full(act, ("o", O))
                    if O > 0:
                        wait_full(act, ("osum", O - 1))
                    A(m1["sq"], bank(("o", O))[:], ACT.Square).then_inc(osq_ready, 1)
                if core:
                    exp_level(G, 3)
                    exp_level(G, 4)
                if new:
                    act.wait_ge(f_ready, H + 1)
                    if H >= 2:
                        act.wait_ge(y_ready, H - 2) if H > 2 else None
                    A(m1["b"][:, H % 2, :], m1["f"], ACT.Ln).then_inc(lf_ready, 1)
                if outp:
                    wait_full(act, ("osum", O))
                    if O > 0:
                        act.wait_ge(y_ready, O)
                    drains(A(m1["rs"], bank(("osum", O))[:], ACT.Ln, bias=eps_t[:, 0:1], scale=1.0 / P), ("osum", O))
                    wait_drained(act, ("osum", O))
                    A(m1["rs"], m1["rs"], ACT.Exp, scale=-0.5).then_inc(rs_ready, 1)
                if core:
                    wait_full(act, ("khT", G))
                    if G > 0:
                        wait_full(act, ("dst", G - 1))
                    drains(A(m1["kh"].rearrange("p a b -> p (a b)"), bank(("khT", G))[:, 0:3 * P], ACT.Copy), ("khT", G))
                    exp_level(G, 5)
                    exp_level(G, 6)
                if new:
                    wait_full(act, ("c", H, 2))
                    drains(A(m1["v"][:, H % 2, :], bank(("c", H, 2))[:], ACT.Copy), ("c", H, 2))
                if core:
                    exp_level(G, 7)
                if new:
                    wait_full(act, ("c", H, 1))
                    if H >= 2:
                        act.wait_ge(qk_ready, (H - 1) * LEVELS)
                        act.wait_ge(qe_ready, H - 1)
                        act.wait_ge(y_ready, H - 1)
                    drains(A(m1["q"][:, H % 2, :], bank(("c", H, 1))[:], ACT.Silu), ("c", H, 1))
                    wait_full(act, ("c", H, 3))
                    drains(A(m1["sg"][:, H % 2, :], bank(("c", H, 3))[:], ACT.Silu), ("c", H, 3))
            moe(1)
            norm(4)
            act.dma_start(me["fin_g"], final_g[None, :].broadcast_to([P, D])).then_inc(final_in, 16)

        @block.gpsimd
        def _(pool):
            g = nc.gpsimd
            st = Steps(pool, pool_step)
            g.memset(eps_t[:], EPS).then_inc(eps_made, 1)
            st.then(g.memset(ident[:], 0.0))
            g.affine_select(out=ident[:], in_=ident[:], compare_op=ALU.not_equal, fill=1.0, base=0,
                            pattern=[[-1, P]], channel_multiplier=1).then_inc(made, 1)
            g.memset(m0["wa"], 0.0).then_inc(diag_zero, 1)
            g.memset(m0["wx"], 0.0).then_inc(diag_zero, 1)

            st.then(g.memset(ones[:], 1.0))
            g.affine_select(out=tri[:], in_=ones[:], compare_op=ALU.is_gt, fill=0.0, base=0,
                            pattern=[[1, P]], channel_multiplier=-1).then_inc(made, 1)
            g.iota(iota[:], [[1, CAP]], base=0, channel_multiplier=0, allow_small_or_imprecise_dtypes=True
                   ).then_inc(made, 1)
            g.iota(gkey[:], [[-1, NG]], base=NG, channel_multiplier=0, allow_small_or_imprecise_dtypes=True
                   ).then_inc(made, 1)
            g.iota(ekey[:], [[-1, NE]], base=NE, channel_multiplier=0, allow_small_or_imprecise_dtypes=True
                   ).then_inc(made, 1)
            g.iota(tokval[:], [[T, 2], [P, NT]], base=1, channel_multiplier=1,
                   allow_small_or_imprecise_dtypes=True).then_inc(made, 1)
            st.then(g.memset(keep[:], 1.0))
            g.memset(keep[:].rearrange("p (a b) -> p a b", a=NT)[:, :, 0:1], 0.0).then_inc(made, 1)
            for L in range(1, LEVELS + 1):
                m = P >> L
                nb = P // (2 * m)
                v = masks[:, L - 1, :].rearrange("p (a b) -> p a b", a=nb)
                st.then(g.memset(masks[:, L - 1, :], 0.0))
                w = v[:, :, m:2 * m]
                st.then(g.memset(w, 1.0))
                st.then(g.affine_select(out=w, in_=w, compare_op=ALU.is_ge, fill=0.0, base=0,
                                        pattern=[[-2 * m, nb], [0, m]], channel_multiplier=1))
                ins = g.affine_select(out=w, in_=w, compare_op=ALU.is_gt, fill=0.0, base=m,
                                      pattern=[[2 * m, nb], [0, m]], channel_multiplier=-1)
                if L < LEVELS:
                    st.then(ins)
                else:
                    ins.then_inc(made, 1)

            def gather_rows(l, j):
                pool.sem_inc(moving, 1)
                g.indirect_dma_start(out=me["rows"][0:CAP, j, :], out_offset=None, in_=xg_d[l],
                                     in_offset=bass.IndirectOffsetOnAxis(ap=gi[j][:, 0:1], axis=0),
                                     bounds_check=T - 1, oob_is_err=False).then_inc(gathered[j], 16)

            def scatter_rows(l, j):
                pool.sem_inc(moving, 1)
                g.indirect_dma_start(out=y_d[l], out_offset=bass.IndirectOffsetOnAxis(ap=si[j][:, 0:1], axis=0),
                                     in_=me["rows"][0:CAP, 2 + j, :], in_offset=None,
                                     bounds_check=2 * T - 1, oob_is_err=False).then_inc(scattered[j], 16)

            def moe(l):
                base = moe_base[l]
                IC = l * 2 * NE
                for n in (0, 1):
                    wait_full(pool, ("out", l, NT - 1, n))
                g.memset(me["rows"][0:CAP, 0:2, :], 0.0).then_inc(pool_rows, 1)
                pool.wait_ge(pool_rows, l + 1)
                pool.wait_ge(table_ready, l * 2 + 2)
                pool.wait_ge(xh_stored, 16 * NT * (l + 1))
                for e in range(2):
                    g.tensor_copy(gi[e][:], xi[:, e:e + 1]).then_inc(idx_copied, 1)
                    pool.wait_ge(idx_copied, IC + e + 1)
                    gather_rows(l, e)

                def step(e, k, j, ahead=True):
                    c = e * 2 + (IC + 2)
                    if ahead:
                        pool.wait_ge(filled[BX], e + (base[BX] + 1))
                        pool.wait_ge(gathered[j], k * 16 + 16 * (l * (NE // 2) + 1))
                        g.tensor_copy(gi[j][:], xi[:, bass.ds(e + 2, 1)]).then_inc(idx_copied, 1)
                        pool.wait_ge(idx_copied, c + 1)
                        gather_rows(l, j)
                    if not (isinstance(k, int) and k == 0):
                        pool.wait_ge(scattered[j], k * 16 + 16 * (l * (NE // 2)))
                    elif l > 0:
                        pool.wait_ge(scattered[j], 16 * l * (NE // 2))
                    g.tensor_copy(si[j][:], ri[:, bass.ds(e, 1)]).then_inc(idx_copied, 1)
                    pool.wait_ge(idx_copied, (c + 2) if ahead else (e + (IC + NE + 1)))
                    for z in range(2):
                        pool.wait_ge(drained[BZ + z], e + (base[BZ + z] + 1))
                    scatter_rows(l, j)

                step(0, 0, 0)
                step(1, 0, 1)
                with pool.Fori(1, NE // 2 - 1) as i:
                    step(i * 2, i, 0)
                    step(i * 2 + 1, i, 1)
                step(NE - 2, NE // 2 - 1, 0, ahead=False)
                step(NE - 1, NE // 2 - 1, 1, ahead=False)
                for j in range(2):
                    pool.wait_ge(scattered[j], 16 * (l + 1) * (NE // 2))
                more_blocks(l)
                pool.sem_inc(ov_done, 1)

            def more_blocks(l):
                pool.wait_ge(flag_ready, l + 1)
                more = pool.value_load(flag[0:1, l:l + 1], min_val=0, max_val=1)
                o, per_e = ov[l], BLOCKS - 1
                with pool.If(more > 0):
                    pool.wait_ge(o["pe"], 1)
                    pool.wait_ge(o["tab"], 2 * per_e)
                    pool.sem_inc(o["scatter"], 16)
                    with pool.Fori(0, NE) as e:
                        with pool.Fori(0, per_e) as b:
                            n = e * per_e + b
                            col = b * NE + e
                            g.tensor_copy(gi[0][:], xio[:, bass.ds(col, 1)]).then_inc(o["idx"], 1)
                            g.tensor_copy(si[0][:], rio[:, bass.ds(col, 1)]).then_inc(o["idx"], 1)
                            pool.wait_ge(o["idx"], n * 2 + 2)
                            pool.wait_ge(o["scatter"], n * 16 + 16)
                            pool.sem_inc(moving, 1)
                            g.indirect_dma_start(out=me["rows"][0:CAP, 0, :], out_offset=None, in_=xg_d[l],
                                                 in_offset=bass.IndirectOffsetOnAxis(ap=gi[0][:, 0:1], axis=0),
                                                 bounds_check=T - 1, oob_is_err=False).then_inc(o["gather"], 16)
                            pool.wait_ge(o["dve"], n * 4 + 4)
                            pool.sem_inc(moving, 1)
                            g.indirect_dma_start(out=y_d[l],
                                                 out_offset=bass.IndirectOffsetOnAxis(ap=si[0][:, 0:1], axis=0),
                                                 in_=me["rows"][0:CAP, 2, :], in_offset=None,
                                                 bounds_check=2 * T - 1, oob_is_err=False).then_inc(o["scatter"], 16)
                    pool.wait_ge(o["scatter"], 16 * (NE * per_e + 1))

            moe(0)

            def mix_level(G, L):
                m = P >> L
                nb = T // (2 * m)
                view = lambda t: t.rearrange("p (a b) -> p a b", a=nb)
                e, qk = view(m1["e"][:, L % 2, :]), view(m1["qk"][:, L % 2, :])
                q, kk = view(m1["q"][:, G % 2, :]), view(m1["kk"][:, G % 2, :])
                pool.wait_ge(e_exp, G * LEVELS + L)
                if L == 1:
                    wait_drained(pool, ("c", G, 1))
                    pool.wait_ge(kk_ready, G + 1)
                if L >= 3:
                    wait_full(pool, ("lev", G, L - 2))
                elif G > 0:
                    wait_full(pool, ("lev", G - 1, L + 4 if L == 2 else 7))
                g.tensor_tensor(qk[:, :, 0:m], kk[:, :, 0:m], e[:, :, 0:m], ALU.mult)
                g.tensor_tensor(qk[:, :, m:2 * m], q[:, :, m:2 * m], e[:, :, m:2 * m], ALU.mult
                                ).then_inc(qk_ready, 1)

            for H in range(HEADS_C + 1):
                new, G = H < HEADS_C, H - 1
                core = G >= 0
                if core:
                    mix_level(G, 1)
                    mix_level(G, 2)
                    pool.wait_ge(dl_exp, G + 1)
                    g.tensor_tensor(m1["dl"], m1["dl"],
                                    m1["kk"][:, G % 2, 0:3 * P].rearrange("p (a b) -> p a b", a=3), ALU.mult
                                    ).then_inc(kh_ready, 1)
                if new:
                    pool.wait_ge(f_ready, H + 1)
                    if H >= 2:
                        wait_full(pool, ("lev", H - 2, 0))
                    g.tensor_scalar(m1["kk"][:, H % 2, :], m1["f"], -1.0, 1.0, ALU.mult, ALU.add).then_inc(kk_ready, 1)
                if core:
                    for L in (3, 4):
                        mix_level(G, L)
                    pool.wait_ge(eb_ready, G + 1)
                    if G >= 2:
                        wait_full(pool, ("o", G - 2))
                    g.tensor_tensor(m1["qe"][:, G % 2, :], m1["q"][:, G % 2, :], m1["eb"], ALU.mult
                                    ).then_inc(qe_ready, 1)
                    for L in (5, 6, 7):
                        mix_level(G, L)
                if new:
                    wait_drained(pool, ("c", H, 3))
                    g.tensor_scalar(m1["sg"][:, H % 2, :], m1["sg"][:, H % 2, :], at["norm_g"][:, H:H + 1], None,
                                    ALU.mult).then_inc(sgg_ready, 1)
            moe(1)

        @block.vector
        def _(dve):
            v = nc.vector
            st = Steps(dve, dve_step)

            def norm_col(n, t):
                dve.wait_ge(std_ready, n * NT + t + 1)
                v.reciprocal(rstd[:, n, t:t + 1], std[:, n, t:t + 1]).then_inc(rstd_ready, 1)

            def norm(n):
                gain = at["mix_g" if n % 2 == 0 else "ffn_g"]
                norm_col(n, 0)
                if n == 0:
                    dve.wait_ge(vec_in, 16)
                for t in range(NT):
                    if t + 1 < NT:
                        norm_col(n, t + 1)
                    for half in range(2):
                        job = ("xt", n, t, half)
                        c0 = (n // 2) * NC + half * 4
                        wait_full(dve, job)
                        drains(v.tensor_tensor(xT[:, half * 4:half * 4 + 4, t * P:(t + 1) * P],
                                               bank(job)[:].rearrange("p (c t) -> p c t", c=4),
                                               gain[:, c0:c0 + 4].unsqueeze(2).broadcast_to([P, 4, P]), ALU.mult), job)

            def add_out(l):
                for nb in range(2):
                    for t in range(NT):
                        job = ("out", l, t, nb)
                        wait_full(dve, job)
                        hh = h[:, t, nb * 512:(nb + 1) * 512]
                        drains(v.tensor_tensor(hh, bank(job)[:], hh, ALU.add), job)

            v.memset(m0["rtab"][0:HEADS_B, 639:640], 0.0).then_inc(rtab_full, 1)
            norm(0)
            v.memset(m0["xa"][:, :, 0:3], 0.0).then_inc(dve_made, 1)
            dve.wait_ge(rtab_in, 16)
            v.tensor_copy(m0["rtab"][0:HEADS_B, 0:255], m0["rtab"][0:HEADS_B, 255:256].broadcast_to([HEADS_B, 255])
                          ).then_inc(rtab_full, 1)
            lam, u, w, acc = at["lam"], lamt[:, 1, :], lamt[:, 2, :], lamt[:, 3, :]
            v.scalar_tensor_tensor(out=lamt[:, 0, :], in0=lam, scalar=-1.0, in1=lam, op0=ALU.mult, op1=ALU.max
                                   ).then_inc(lam_in, 1)
            st.then(v.tensor_tensor(lb[:], at["lb0"], at["lb1"], ALU.max))
            v.tensor_tensor(lbt[:, 0, :], at["lb0"], lb[:], ALU.subtract).then_inc(lb_in, 1)
            v.tensor_tensor(lbt[:, 1, :], at["lb1"], lb[:], ALU.subtract).then_inc(lb_in, 1)
            dve.wait_ge(lam_exp, 1)
            st.then(v.tensor_scalar(w, u, 2.0, None, ALU.add))
            st.then(v.reciprocal(w, w))
            st.then(v.tensor_tensor(u, u, w, ALU.mult))
            st.then(v.tensor_tensor(w, u, u, ALU.mult))
            st.then(v.tensor_scalar(acc, w, 1.0 / 17, 1.0 / 15, ALU.mult, ALU.add))
            for k in (13, 11, 9, 7, 5, 3, 1):
                st.then(v.tensor_tensor(acc, acc, w, ALU.mult))
                st.then(v.tensor_scalar(acc, acc, 1.0 / k, None, ALU.add))
            st.then(v.tensor_tensor(acc, acc, u, ALU.mult))
            st.then(v.tensor_scalar(w, lam, 0.0, 0.5, ALU.min, ALU.mult))
            st.then(v.tensor_tensor(acc, w, acc, ALU.subtract))
            v.tensor_scalar(cl[:, 0, :], acc, 16.0, None, ALU.mult).then_inc(cl_ready, 1)
            v.tensor_scalar(cl[:, 1, :], acc, -16.0, None, ALU.mult).then_inc(cl_ready, 1)

            dve.wait_ge(dve_made, 1)
            for m in range(4):
                wait_drained(dve, ("xa", m))
                xc = m0["xc"][:, m, :]
                taps = [at["conv_w"][:, 4 * m + j:4 * m + j + 1] for j in range(CONV)]
                st.then(v.tensor_scalar(xc, m0["xa"][:, m, 0:T], taps[0], at["conv_b"][:, m:m + 1], ALU.mult, ALU.add))
                for j in (1, 2, 3):
                    ins = v.scalar_tensor_tensor(out=xc, in0=m0["xa"][:, m, j:j + T], scalar=taps[j], in1=xc,
                                                 op0=ALU.mult, op1=ALU.add)
                    if j < 3:
                        st.then(ins)
                    else:
                        ins.then_inc(xc_ready, 1)
            dve.wait_ge(xc_ready, 4)
            ga, gx = m0["ga"], m0["xa"][:, :, 0:T]
            for m in range(4):
                wait_drained(dve, ("ga", m))
            st.then(v.tensor_tensor(gx, ga, ga, ALU.mult))
            st.then(v.tensor_scalar(gx, gx, GELU_A, 1.0, ALU.mult, ALU.add))
            v.tensor_tensor(gx, gx, ga, ALU.mult).then_inc(gelu_in, 1)
            for m in range(4):
                job = ("q", m)
                wait_full(dve, job)
                drains(v.tensor_scalar(m0["q"][:, m, :].rearrange("p (i t) -> p i t", i=NT)[:, :, ::-1],
                                       bank(job)[:].rearrange("p (i t) -> p i t", i=NT), 0.125, None, ALU.mult), job)
            for m in range(4):
                wait_drained(dve, ("ix", m))
                wait_drained(dve, ("ra", m))
            v.tensor_tensor(m0["i"], m0["i"], m0["xc"], ALU.mult).then_inc(rg_x, 1)
            dve.wait_ge(rg_a, 4)
            dve.wait_ge(rg_x, 1)
            st.then(v.tensor_tensor(m0["xc"], m0["a"], m0["a"], ALU.mult))
            dve.wait_ge(rg_t, 4)
            v.scalar_tensor_tensor(out=m0["xc"], in0=m0["xc"], scalar=1.0, in1=m0["r"], op0=ALU.add, op1=ALU.mult
                                   ).then_inc(rg_m2, 1)
            dve.wait_ge(gelu_t, 1)
            st.then(v.scalar_tensor_tensor(out=gx, in0=gx, scalar=1.0, in1=ga, op0=ALU.add, op1=ALU.mult))
            dve.wait_ge(rg_m, 1)
            st.then(v.tensor_tensor(m0["i"], m0["i"], m0["xc"], ALU.mult))
            for m in range(4):
                st.then(v.tensor_tensor_scan(m0["r"][:, m, :], m0["a"][:, m, :], m0["i"][:, m, :], 0.0,
                                             ALU.mult, ALU.add))
            dve.wait_ge(rtab_out, 16)
            v.scalar_tensor_tensor(out=m0["y"][:, 0:4, :], in0=gx, scalar=0.5, in1=m0["r"], op0=ALU.mult,
                                   op1=ALU.mult).then_inc(ya_ready, 1)

            for n in range(NA + 3):
                if n < NA:
                    hd, N = n // NT, (n % NT + 1) * P
                    if n % NT == 0:
                        dve.wait_ge(strip_in[hd % 2], 16 * (hd // 2 + 1))
                        v.memset(m0["strip"][64:128, hd % 2, T - 64:T], -1e30).then_inc(strip_ready, 1)
                        dve.wait_ge(strip_ready, hd + 1)
                    wait_full(dve, ("S", n))
                    if n >= 3:
                        wait_full(dve, ("T", n - 3))
                    drains(v.tensor_tensor_reduce(m0["s"][:, n % 3, 0:N], bank(("S", n))[:, 0:N],
                                                  m0["strip"][:, hd % 2, T - N:T], 1.0, 0.0, ALU.add, ALU.max,
                                                  m0["mx"][:, n:n + 1]), ("S", n))
                if 1 <= n <= NA:
                    q = n - 1
                    N = (q % NT + 1) * P
                    dve.wait_ge(prob_exp, q + 1)
                    st.then(v.reciprocal(m0["rs"][:, q:q + 1], m0["sum"][:, q:q + 1]))
                    v.tensor_scalar(m0["s"][:, q % 3, 0:N], m0["s"][:, q % 3, 0:N], m0["rs"][:, q:q + 1], None,
                                    ALU.mult).then_inc(prob_ready, 1)
                if n < NA:
                    wait_drained(dve, ("S", n))
                    v.tensor_scalar(m0["nmx"][:, n:n + 1], m0["mx"][:, n:n + 1], -1.0, None, ALU.mult
                                    ).then_inc(score_max, 1)
                if n >= 3:
                    q = n - 3
                    hd, i, lo = q // NT, q % NT, 64 * (q // NT % 2)
                    wait_full(dve, ("O", q))
                    drains(v.tensor_copy(m0["y"][lo:lo + 64, 4 + hd // 2, i * P:(i + 1) * P][:, ::-1],
                                         bank(("O", q))[lo:lo + 64, 0:P]), ("O", q))
            add_out(0)

            def route(l):
                lg, em, key, M0, M1, M = (me[k] for k in ("lg", "em", "key", "M0", "M1", "M"))
                g4, goh, ex, w, pos = me["g4"], me["goh"], me["ex"], me["w"], me["pos"]
                wt = lambda i: w[:, i, :]
                one = lambda a, n: a.unsqueeze(2).broadcast_to([P, NT, n])
                row = lambda a, n: a[:].unsqueeze(1).broadcast_to([P, NT, n])
                job = ("lg", l)
                if l == 0:
                    dve.wait_ge(made, 8)
                wait_full(dve, job)
                drains(v.tensor_copy(lg, bank(job)[:, 0:256].rearrange("p (t n) -> p t n", t=NT)[:, :, 0:NG + NE]), job)
                wait_drained(dve, job)
                st.then(v.tensor_reduce(wt(0), lg[:, :, 0:NG], AX.X, ALU.max))
                st.then(v.tensor_tensor(g4, lg[:, :, 0:NG], one(wt(0), NG), ALU.is_equal))
                st.then(v.tensor_tensor(g4, g4, row(gkey, NG), ALU.mult))
                st.then(v.tensor_reduce(wt(1), g4, AX.X, ALU.max))
                st.then(v.tensor_tensor(goh, g4, one(wt(1), NG), ALU.is_equal))
                by_group = lambda a: a.rearrange("p t (g k) -> p t g k", g=NG)
                spread = lambda a: a.unsqueeze(3).broadcast_to([P, NT, NG, NPG])
                le = lg[:, :, NG:NG + NE]
                for t in range(NT):
                    sp4 = goh[:, t, :].unsqueeze(2).broadcast_to([P, NG, NPG])
                    ins = v.tensor_tensor(em[:, t, :].rearrange("p (g k) -> p g k", g=NG),
                                          le[:, t, :].rearrange("p (g k) -> p g k", g=NG), sp4, ALU.mult)
                st.then(ins)
                st.then(v.tensor_scalar(g4, goh, 1e30, -1e30, ALU.mult, ALU.add))
                for t in range(NT):
                    sp4 = g4[:, t, :].unsqueeze(2).broadcast_to([P, NG, NPG])
                    e4 = em[:, t, :].rearrange("p (g k) -> p g k", g=NG)
                    ins = v.tensor_tensor(e4, e4, sp4, ALU.add)
                st.then(ins)
                for k, dst in ((0, M0), (1, M1)):
                    st.then(v.tensor_reduce(wt(2 + k), em, AX.X, ALU.max))
                    st.then(v.tensor_tensor(key, em, one(wt(2 + k), NE), ALU.is_equal))
                    st.then(v.tensor_tensor(key, key, row(ekey, NE), ALU.mult))
                    st.then(v.tensor_reduce(wt(4), key, AX.X, ALU.max))
                    st.then(v.tensor_tensor(dst, key, one(wt(4), NE), ALU.is_equal))
                    if k == 0:
                        st.then(v.scalar_tensor_tensor(out=em, in0=M0, scalar=-1e31, in1=em, op0=ALU.mult, op1=ALU.add))
                v.tensor_tensor(M, M0, M1, ALU.add).then_inc(one_hot, 1)
                st.then(v.tensor_tensor(ex[:, :, 0:NG], lg[:, :, 0:NG], one(wt(0), NG), ALU.subtract))
                v.tensor_tensor(ex[:, :, NG], wt(3), wt(2), ALU.subtract).then_inc(route_in, 1)
                job = ("pos", l)
                for k, Mk in ((0, M0), (1, M1)):
                    if k == 0:
                        wait_full(dve, job)
                    st.then(v.tensor_tensor(em, bank(job)[:, 0:NT * NE].rearrange("p (t n) -> p t n", t=NT), Mk, ALU.mult))
                    st.then(v.tensor_reduce(pos[:, k, :], em, AX.X, ALU.add))
                for k, Mk in ((0, M0), (1, M1)):
                    st.then(v.tensor_tensor(me["B"][:, k, :, :], Mk, one(tokval[:, k, :], NE), ALU.mult))
                    ins = v.tensor_tensor(me["A"][:, k, :, :], row(iota, CAP), one(pos[:, k, :], CAP), ALU.is_equal)
                    if k == 0:
                        st.then(ins)
                    else:
                        ins.then_inc(slots_hot, 1)
                drains(v.tensor_reduce(w[:, 5, 0:1], bank(job)[:, 256:256 + NE], AX.X, ALU.max), job)
                wait_drained(dve, job)
                v.tensor_scalar(flag[:, l:l + 1], w[:, 5, 0:1], CAP + 0.5, None, ALU.is_gt).then_inc(flag_ready, 1)
                job = ("tab", l)
                wait_full(dve, job)
                tab = me["tab"][0:CAP, :, :]
                drains(v.tensor_copy(tab[:, 0, :], bank(job)[0:CAP, 0:NE]), job)
                wait_drained(dve, job)
                st.then(v.tensor_scalar(tab[:, 1, :], tab[:, 0, :], 0.0, OFF, ALU.is_equal, ALU.mult))
                st.then(v.scalar_tensor_tensor(out=tab[:, 1, :], in0=tab[:, 0, :], scalar=-1.0, in1=tab[:, 1, :],
                                               op0=ALU.add, op1=ALU.add))
                st.then(v.tensor_scalar(tab[:, 2, :], tab[:, 0, :], T + 0.5, -float(T), ALU.is_gt, ALU.mult))
                v.tensor_copy(ri[:], tab[:, 1, :]).then_inc(table_ready, 1)
                v.tensor_tensor(xi[:], tab[:, 1, :], tab[:, 2, :], ALU.add).then_inc(table_ready, 1)
                dve.wait_ge(route_exp, l + 1)
                st.then(v.tensor_reduce(wt(6), ex[:, :, 0:NG], AX.X, ALU.add))
                st.then(v.tensor_scalar(wt(7), ex[:, :, NG], 1.0, None, ALU.add))
                st.then(v.tensor_tensor(wt(6), wt(6), wt(7), ALU.mult))
                st.then(v.reciprocal(gates[:, 0, :], wt(6)))
                st.then(v.tensor_tensor(gates[:, 1, :], gates[:, 0, :], ex[:, :, NG], ALU.mult))

            def times_gain(l, dst):
                g8 = at["ffn_g"][:, l * NC:(l + 1) * NC].unsqueeze(2).broadcast_to([P, NC, CAP])
                return v.tensor_tensor(dst.rearrange("p (c t) -> p c t", c=NC),
                                       ps[BX][:].rearrange("p (c t) -> p c t", c=NC), g8, ALU.mult)

            def turned(l, e, j):
                base = moe_base[l]
                dve.wait_ge(filled[BX], e + (base[BX] + 1))
                if not (isinstance(e, int) and e < 2):
                    dve.wait_ge(filled[BU], e + (base[BU] - 1))
                times_gain(l, me["xgT"][:, j, :]).then_inc(drained[BX], 1)

            def half_rows(l, e, k, j):
                base = moe_base[l]
                dve.wait_ge(filled[BZ], e + (base[BZ] + 1))
                if not (isinstance(k, int) and k == 0):
                    dve.wait_ge(scattered[j], k * 16 + 16 * l * (NE // 2))
                v.tensor_copy(me["rows"][0:CAP, 2 + j, 0:512], ps[BZ][0:CAP, :]).then_inc(drained[BZ], 1)

            def dve_expert(l, e, k, j, first=False, last=False):
                base = moe_base[l]
                dve.wait_ge(filled[BU], e + (base[BU] + 1))
                dve.wait_ge(drained[BG], e + (base[BG] + 1))
                if not (isinstance(e, int) and e < 2):
                    dve.wait_ge(filled[BY], e + (base[BY] - 1))
                v.tensor_tensor(me["hT"][:, j, :], me["silu"][:, j, :], ps[BU][:, 0:FC * CAP], ALU.mult
                                ).then_inc(hidden, 1)
                dve.wait_ge(hidden, e + (l * NE + 1))
                dve.sem_inc(drained[BU], 1)
                if not last:
                    turned(l, e + 1, 1 - j)
                if not first:
                    half_rows(l, e - 1, k - 1 + j, 1 - j)

            def more_blocks(l):
                dve.wait_ge(flag_ready, l + 1)
                more = dve.value_load(flag[0:1, l:l + 1], min_val=0, max_val=1)
                o, per_e = ov[l], BLOCKS - 1
                s2 = o["step"]
                with dve.If(more > 0):
                    dve.wait_ge(o["pe"], 1)
                    tab = me["tab"][0:CAP, :, :]
                    with dve.Fori(0, per_e) as b:
                        so = Steps(dve, s2)
                        so.base = b * 5
                        so.then(v.tensor_scalar(iota[:], iota[:], float(CAP), None, ALU.add))
                        for k in range(2):
                            ins = v.tensor_tensor(me["A"][:, k, :, :], iota[:].unsqueeze(1).broadcast_to([P, NT, CAP]),
                                                  me["pos"][:, k, :].unsqueeze(2).broadcast_to([P, NT, CAP]),
                                                  ALU.is_equal)
                        ins.then_inc(o["tab"], 1)
                        dve.wait_ge(o["tabpe"], b + 1)
                        so.then(v.tensor_copy(tab[:, 0, :], ps[6][0:CAP, 0:NE]))
                        so.then(v.tensor_scalar(tab[:, 1, :], tab[:, 0, :], 0.0, OFF, ALU.is_equal, ALU.mult))
                        so.then(v.scalar_tensor_tensor(out=tab[:, 1, :], in0=tab[:, 0, :], scalar=-1.0,
                                                       in1=tab[:, 1, :], op0=ALU.add, op1=ALU.add))
                        so.then(v.tensor_scalar(tab[:, 2, :], tab[:, 0, :], T + 0.5, -float(T), ALU.is_gt, ALU.mult))
                        v.tensor_copy(rio[:, bass.ds(b * NE, NE)], tab[:, 1, :])
                        v.tensor_tensor(xio[:, bass.ds(b * NE, NE)], tab[:, 1, :], tab[:, 2, :], ALU.add
                                        ).then_inc(o["tab"], 1)
                        dve.wait_ge(o["tab"], b * 2 + 2)
                    v.tensor_scalar(iota[:], iota[:], -float(CAP * per_e), None, ALU.add).then_inc(s2, 1)
                    dve.wait_ge(s2, per_e * 5 + 1)
                    with dve.Fori(0, NE * per_e) as n:
                        dve.wait_ge(o["pe"], n * 5 + 2)
                        times_gain(l, me["xgT"][:, 0, :]).then_inc(o["dve"], 1)
                        dve.wait_ge(o["pe"], n * 5 + 4)
                        dve.wait_ge(o["act"], n * 2 + 1)
                        v.tensor_tensor(me["hT"][:, 0, :], me["silu"][:, 0, :], ps[BU][:, 0:FC * CAP], ALU.mult
                                        ).then_inc(o["dve"], 1)
                        dve.wait_ge(o["pe"], n * 5 + 6)
                        for z in range(2):
                            v.tensor_copy(me["rows"][0:CAP, 2, z * 512:(z + 1) * 512], ps[BZ + z][0:CAP, :]
                                          ).then_inc(o["dve"], 1)

            def combine(l):
                for t in range(NT):
                    j = t % 2
                    dve.wait_ge(yrow_in[j], 32 * (2 * l + t // 2 + 1))
                    for k in range(2):
                        v.scalar_tensor_tensor(out=h[:, t, :], in0=me["rows"][:, 2 * j + k, :],
                                               scalar=gates[:, k, t:t + 1], in1=h[:, t, :], op0=ALU.mult,
                                               op1=ALU.add).then_inc(h_ready, 1)
                        dve.wait_ge(h_ready, l * 2 * NT + 2 * t + k + 1)

            def moe(l):
                norm(2 * l + 1)
                route(l)
                turned(l, 0, 0)
                dve_expert(l, 0, 0, 0, first=True)
                dve_expert(l, 1, 0, 1)
                dve_expert(l, 2, 1, 0)
                with dve.Fori(1, NE // 2 - 1) as i:
                    dve_expert(l, i * 2 + 1, i, 1)
                    dve_expert(l, i * 2 + 2, i + 1, 0)
                dve_expert(l, NE - 1, NE // 2 - 1, 1, last=True)
                half_rows(l, NE - 1, NE // 2 - 1, 1)
                more_blocks(l)
                combine(l)

            dve.wait_ge(lb_exp, 1)
            st.then(v.tensor_tensor(lbt[:, 0, :], lbt[:, 2, :], lbt[:, 3, :], ALU.add))
            st.then(v.reciprocal(lbt[:, 0, :], lbt[:, 0, :]))
            st.then(v.tensor_tensor(lb[:], lbt[:, 2, :], lbt[:, 0, :], ALU.mult))
            st.then(v.tensor_scalar(oml[:], lb[:], -1.0, 1.0, ALU.mult, ALU.add))
            moe(0)

            norm(2)

            def sub_level(G, L):
                m = P >> L
                nb = T // (2 * m)
                b = m1["b"][:, G % 2, :].rearrange("p (a b) -> p a b", a=nb)
                e = m1["e"][:, L % 2, :].rearrange("p (a b) -> p a b", a=nb)
                mid = b[:, :, m - 1:m].broadcast_to([P, nb, m])
                if L == 1:
                    dve.wait_ge(b_ready, G + 1)
                last = G * LEVELS + L - 2 if L > 2 else G * LEVELS + (0 if L == 1 else -1)
                if last > 0:
                    dve.wait_ge(qk_ready, last)
                v.tensor_tensor(e[:, :, 0:m], mid, b[:, :, 0:m], ALU.subtract)
                v.tensor_tensor(e[:, :, m:2 * m], b[:, :, m:2 * m], mid, ALU.subtract).then_inc(e_sub, 1)

            def take_level(G, L):
                job = ("lev", G, L)
                src = bank(job)[:].rearrange("p (a b) -> p a b", a=NT)
                dst = m1["attn"][:, G % 2, :].rearrange("p (a b) -> p a b", a=NT)
                wait_full(dve, job)
                if L == 0:
                    if G >= 2:
                        wait_full(dve, ("o", G - 2))
                    drains(v.tensor_tensor(dst, src, ident[:].unsqueeze(1).broadcast_to([P, NT, P]), ALU.mult), job)
                else:
                    wait_drained(dve, ("lev", G, L - 1))
                    drains(v.copy_predicated(dst, masks[:, L - 1, :].bitcast(U32).unsqueeze(1).broadcast_to([P, NT, P]), src), job)

            for H in range(HEADS_C + 2):
                new, G, O = H < HEADS_C, H - 1, H - 2
                core, outp = 0 <= G < HEADS_C, O >= 0
                if core:
                    sub_level(G, 1)
                    sub_level(G, 2)
                    b3 = m1["b"][:, G % 2, 0:3 * P].rearrange("p (a b) -> p a b", a=3)
                    if G > 0:
                        wait_full(dve, ("khT", G - 1))
                    v.tensor_tensor(m1["dl"], b3[:, :, P - 1:P].broadcast_to([P, 3, P]), b3, ALU.subtract
                                    ).then_inc(dl_sub, 1)
                    take_level(G, 0)
                if new:
                    wait_drained(dve, ("c", H, 0))
                    v.tensor_scalar(m1["f"], m1["f"], oml[:, H:H + 1], lb[:, H:H + 1], ALU.mult, ALU.add
                                    ).then_inc(f_ready, 1)
                if core:
                    sub_level(G, 3)
                    take_level(G, 1)
                    sub_level(G, 4)
                    take_level(G, 2)
                if new:
                    dve.wait_ge(lf_ready, H + 1)
                    b = m1["b"][:, H % 2, :]
                    v.tensor_tensor_scan(b, keep[:], b, 0.0, ALU.mult, ALU.add).then_inc(b_ready, 1)
                if outp:
                    dve.wait_ge(rs_ready, O + 1)
                    wait_full(dve, ("o", O))
                    drains(v.tensor_tensor(m1["rs"], bank(("o", O))[:], m1["rs"], ALU.mult), ("o", O))
                    wait_drained(dve, ("o", O))
                    dve.wait_ge(sgg_ready, O + 1)
                    v.tensor_tensor(m1["y"][:, O, :], m1["rs"], m1["sg"][:, O % 2, :], ALU.mult).then_inc(y_ready, 1)
                if core:
                    sub_level(G, 5)
                    take_level(G, 3)
                    sub_level(G, 6)
                    take_level(G, 4)
                    job = ("dst", G)
                    wait_full(dve, job)
                    dve.wait_ge(eb_ready, G + 1)
                    if G >= 2:
                        wait_full(dve, ("o", G - 2))
                    stt, src = m1["st"][:, G % 2, :], bank(job)
                    st.then(v.tensor_copy(stt[:, 0:P], src[:, 0:P]))
                    st.then(v.scalar_tensor_tensor(out=stt[:, P:2 * P], in0=stt[:, 0:P],
                                                   scalar=m1["eb"][:, 2 * P - 1:2 * P], in1=src[:, P:2 * P],
                                                   op0=ALU.mult, op1=ALU.add))
                    drains(v.scalar_tensor_tensor(out=stt[:, 2 * P:3 * P], in0=stt[:, P:2 * P],
                                                  scalar=m1["eb"][:, 3 * P - 1:3 * P], in1=src[:, 2 * P:3 * P],
                                                  op0=ALU.mult, op1=ALU.add), job)
                    sub_level(G, 7)
                    take_level(G, 5)
                    take_level(G, 6)
                    take_level(G, 7)
            add_out(1)
            moe(1)
            for t in range(NT):
                norm_col(4, t)
            dve.wait_ge(final_in, 16)
            for t in range(NT):
                dve.wait_ge(xh_ready, 4 * NT + t + 1)
                v.tensor_tensor(xh[:, t, :], xh[:, t, :], me["fin_g"], ALU.mult).then_inc(out_ready, 1)

    return nc


def kernel(**inputs):
    import numpy as _np
    import concourse.bacc as _bacc
    from concourse import mybir as _mybir
    from concourse.bass_utils import run_bass_kernel_spmd as _run

    a = {k: _np.asarray(v) for k, v in inputs.items()}

    def chunks(vector):
        return vector.reshape(-1, P).T

    cols = _np.concatenate(
        [chunks(a["norm_mix_g"][l]) for l in range(2)] + [chunks(a["norm_ffn_g"][l]) for l in range(2)]
        + [a["ab_conv_w"][0].reshape(CONV, 4, P).transpose(2, 1, 0).reshape(P, 4 * CONV)]
        + [chunks(a[k][0]) for k in ("ab_conv_b", "rg_b_a", "rg_b_x", "rg_lambda")]
        + [chunks(a["c_lb_logits"][i]) for i in range(2)] + [chunks(a["c_norm_g"][0])], axis=1)
    router = _np.concatenate([a["moe_router_group"], a["moe_router_expert"]], axis=2)
    router = router.reshape(2, NC, P, NG + NE).transpose(2, 0, 1, 3).reshape(P, -1)
    c_in = a["c_w_in"][0].reshape(NC, P, 4, HEADS_C, P)[:, :, [1, 0, 2, 3]].transpose(3, 1, 0, 2, 4)
    feeds = {
        "x": a["x"], "cols": cols, "final_g": a["norm_final_g"], "ab_w_in": a["ab_w_in"], "rg_w_a": a["rg_w_a"],
        "rg_w_x": a["rg_w_x"], "bias_rev": a["attn_rel_bias"][0][:, ::-1], "ab_w_out": a["ab_w_out"],
        "c_w_in": c_in.reshape(HEADS_C, P, -1), "c_w_out": a["c_w_out"], "router": router,
        "w_gate": a["moe_w_gate"], "w_up": a["moe_w_up"], "w_down": a["moe_w_down"],
    }
    nc = _bacc.Bacc("TRN2", target_bir_lowering=False, num_devices=1)
    arrays, args = {}, []
    for name, value in feeds.items():
        value = _np.ascontiguousarray(value)
        arrays[f"in_{name}_dram"] = value
        args.append(nc.dram_tensor(f"in_{name}_dram", value.shape, _mybir.dt.from_np(value.dtype),
                                   kind="ExternalInput").ap())
    out = nc.dram_tensor("out_dram", (1, T, D), F32, kind="ExternalOutput").ap()
    trunk(nc, *args, out)
    r = _run(nc, [arrays], core_ids=[0])
    return r.results[0]["out_dram"]
```

```python
from contextlib import ExitStack

import numpy as np

import concourse.bass as bass
from concourse import mybir

ALU = mybir.AluOpType
ACT = mybir.ActivationFunctionType
AX = mybir.AxisListType
F32 = mybir.dt.float32
U32 = mybir.dt.uint32
I32 = mybir.dt.int32

P = 128
D = 1024
T = 512
NT = T // P
NC = D // P
EPS = 1e-6
HEADS_B = 8
AW = 512
CONV = 4
CLIP = 256
HEADS_C = 8
LEVELS = 7
NG, NPG = 4, 8
NE = NG * NPG
F = 512
FC = F // P
CAP = 64
BLOCKS = T // CAP
OFF = float(1 << 20)
GELU_A, GELU_B = 0.044715, 0.7978845608028654

COLS = [("mix_g", 2 * NC), ("ffn_g", 2 * NC), ("conv_w", 4 * CONV), ("conv_b", 4), ("b_a", 4), ("b_x", 4),
        ("lam", 4), ("lb0", 8), ("lb1", 8), ("norm_g", 8)]


class Banks:

    def __init__(self, count):
        self.uses = [0] * count
        self.jobs = {}

    def add(self, job, bank):
        self.jobs[job] = (bank, self.uses[bank])
        self.uses[bank] += 1


class Steps:

    def __init__(self, eng, sem):
        self.eng, self.sem, self.base, self.n = eng, sem, 0, 0

    def then(self, ins):
        self.n += 1
        ins.then_inc(self.sem, 1)
        self.eng.wait_ge(self.sem, self.base + self.n)


def trunk(nc, x, cols, final_g, ab_w_in, rg_w_a, rg_w_x, bias_rev, ab_w_out, c_w_in, c_w_out, router,
          w_gate, w_up, w_down, out):
    with ExitStack() as ctx:
        def sb(name, shape, dt=F32):
            return ctx.enter_context(nc.sbuf_tensor("sb_" + name, shape, dt))

        def sem(name):
            return ctx.enter_context(nc.semaphore(name))

        h = sb("h", [P, NT, D])
        xh = sb("xh", [P, NT, D])
        xT = sb("xT", [P, NC, T])
        ident = sb("ident", [P, P])
        tri = sb("tri", [P, P])
        ones = sb("ones", [P, P])
        iota = sb("iota", [P, CAP])
        gkey = sb("gkey", [P, NG])
        ekey = sb("ekey", [P, NE])
        tokval = sb("tokval", [P, 2, NT])
        masks = sb("masks", [P, LEVELS, P])
        keep = sb("keep", [P, T])
        vec = sb("vec", [P, sum(n for _, n in COLS)])
        rt = sb("rt", [P, 2, NC, NG + NE])
        eps_t = sb("eps_t", [P, 1])
        warm = sb("warm", [P, 1])
        ss = sb("ss", [P, 5, NT])
        std = sb("std", [P, 5, NT])
        rstd = sb("rstd", [P, 5, NT])
        ring_a = sb("ring_a", [P, 3, 8 * 512])
        ring_b = sb("ring_b", [P, 3, 8 * 512])
        ri = sb("ri", [CAP, NE], U32)
        gi = sb("gi", [CAP, 1], U32)
        si = [sb(f"si{j}", [CAP, 1], U32) for j in range(2)]
        xio = sb("xio", [CAP, BLOCKS * NE], U32)
        rio = sb("rio", [CAP, BLOCKS * NE], U32)
        flag = sb("flag", [P, 2], I32)
        gates = sb("gates", [P, 2, NT])
        lamt = sb("lamt", [P, 4, 4])
        cl = sb("cl", [P, 2, 4])
        lbt = sb("lbt", [P, 4, 8])
        lb = sb("lb", [P, 8])
        oml = sb("oml", [P, 8])
        scr = sb("scr", [P, 12960])
        y_d = [nc.dram_tensor(f"expert_rows{l}", [2 * T, D], F32).ap() for l in range(2)]
        xg_d = [nc.dram_tensor(f"norm_rows{l}", [T, D], F32).ap() for l in range(2)]
        bias_d = nc.dram_tensor("bias_rows", [HEADS_B, 640], F32).ap()
        ps = [ctx.enter_context(nc.psum_tensor(f"ps{b}", [P, 512], F32)) for b in range(8)]

        at, o = {}, 0
        for name, n in COLS:
            at[name] = vec[:, o:o + n]
            o += n

        def flat(t):
            return t[:, :, :].rearrange("p a b -> p (a b)")

        def carve(base, sizes):
            views, pos = {}, 0
            for name, shape in sizes:
                n = int(np.prod(shape))
                v = base[:, pos:pos + n]
                if len(shape) == 2:
                    v = v.rearrange("p (a b) -> p a b", a=shape[0])
                elif len(shape) == 3:
                    v = v.rearrange("p (a b c) -> p a b c", a=shape[0], b=shape[1])
                views[name] = v
                pos += n
            assert pos <= base.shape[1], (pos, base.shape)
            return views

        m0 = carve(scr[:], [("y", (8, T)), ("q", (4, T)), ("k", (4, T)), ("strip", (2, T)), ("mx", (32,)),
                            ("nmx", (32,)), ("sum", (32,)), ("rs", (32,)), ("s", (3, T)), ("pt", (2, T)),
                            ("wa", (4, P)), ("wx", (4, P))])
        m0.update(carve(flat(ring_b), [("ga", (4, T)), ("xc", (4, T)), ("r", (4, T)), ("i", (4, T)), ("a", (4, T)),
                                       ("v", (4, T))]))
        m0.update(carve(flat(xh), [("xa", (4, T + 4))]))
        m0.update(carve(scr[:], [("rtab", (640,))]))
        m1 = carve(scr[:], [("q", (2, T)), ("kk", (2, T)), ("b", (2, T)), ("v", (2, T)), ("sg", (2, T)),
                            ("f", (T,)), ("e", (2, T)), ("qk", (2, T)), ("attn", (2, T)), ("eb", (T,)),
                            ("qe", (2, T)), ("dl", (3, P)), ("kh", (3, P)), ("st", (2, 3 * P)), ("sq", (T,)),
                            ("rs", (T,))])
        m1.update(carve(flat(xh), [("y", (8, T))]))
        me = carve(scr[:], [("rows", (4, D)), ("xgT", (2, NC * CAP)), ("hT", (FC * CAP,)), ("silu", (2, F)),
                            ("hrow", (F,)), ("lg", (NT, NG + NE)), ("em", (NT, NE)), ("key", (NT, NE)),
                            ("M0", (NT, NE)), ("M1", (NT, NE)), ("M", (NT, NE)), ("pos", (2, NT)),
                            ("A", (2, NT, CAP)), ("B", (2, NT, NE)), ("g4", (NT, NG)), ("goh", (NT, NG)),
                            ("ex", (NT, 5)), ("tab", (3, NE)), ("w", (12, NT)), ("fin_g", (D,)),
                            ("lgT", (T,)), ("Msum", (NT, NE)),
                            ("sel", (2, NT * CAP)), ("picked", (512,)), ("slots", (NT, NE)), ("slot", (2, NT))])

        yrows = flat(ring_b)[:, 0:2 * NT * D].rearrange("p (a d) -> p a d", d=D)

        filled = [sem(f"filled{b}") for b in range(8)]
        drained = [sem(f"drained{b}") for b in range(8)]
        ring_in = {(r, s): sem(f"ring_in_{r}{s}") for r in "ab" for s in range(3)}
        x_in = [sem(f"x_in{t}") for t in range(NT)]
        vec_in, diag_in, router_in, final_in = (sem(n) for n in ("vec_in", "diag_in", "router_in", "final_in"))
        rtab_in, rtab_full, rtab_out, strip_ready = (sem(n) for n in ("rtab_in", "rtab_full", "rtab_out",
                                                                      "strip_ready"))
        strip_in = [sem(f"strip_in{j}") for j in range(2)]
        made, dve_made, diag_zero, eps_made = (sem(n) for n in ("made", "dve_made", "diag_zero", "eps_made"))
        dve_step, pool_step = sem("dve_step"), sem("pool_step")
        lam_in, lam_exp, cl_ready, lb_in, lb_exp = (sem(n) for n in ("lam_in", "lam_exp", "cl_ready", "lb_in",
                                                                     "lb_exp"))
        ss_ready, std_ready, rstd_ready, xh_ready, h_ready = (sem(n) for n in ("ss_ready", "std_ready", "rstd_ready",
                                                                               "xh_ready", "h_ready"))
        out_ready, out_stored = sem("out_ready"), sem("out_stored")
        xc_ready, rg_x, rg_a, rg_t, rg_m2, rg_m, gelu_in, gelu_t, ya_ready = (
            sem(n) for n in ("xc_ready", "rg_x", "rg_a", "rg_t", "rg_m2", "rg_m", "gelu_in", "gelu_t", "ya_ready"))
        score_max, prob_exp, prob_ready = sem("score_max"), sem("prob_exp"), sem("prob_ready")
        (f_ready, kk_ready, lf_ready, b_ready, sgg_ready, e_sub, e_exp, qk_ready, eb_ready, dl_sub, dl_exp, qe_ready,
         kh_ready, osq_ready, rs_ready, y_ready) = (
            sem(n) for n in ("f_ready", "kk_ready", "lf_ready", "b_ready", "sgg_ready", "e_sub", "e_exp", "qk_ready",
                             "eb_ready", "dl_sub", "dl_exp", "qe_ready", "kh_ready", "osq_ready", "rs_ready",
                             "y_ready"))
        (route_in, route_exp, one_hot, slots_hot, table_ready, flag_ready) = (
            sem(n) for n in ("route_in", "route_exp", "one_hot", "slots_hot", "table_ready",
                             "flag_ready"))
        pool_rows = sem("pool_rows")
        ov_done = sem("more_done")
        moving = sem("moving")
        turning = sem("turning")
        silu_ready, half_out = sem("silu_ready"), sem("half_out")
        idx_copied = sem("idx_copied")
        xh_stored = [sem(f"xh_stored{l}") for l in range(2)]
        col_ready, sel_ready = sem("col_ready"), sem("sel_ready")
        scattered = [sem(f"scattered{j}") for j in range(2)]
        yrow_in = [sem(f"yrow_in{t}") for t in range(NT)]
        rsum_ready, act_step = sem("rsum_ready"), sem("act_step")
        ov = [{k: sem(f"more{l}_{k}") for k in ("w", "pe", "dve", "act", "idx", "gather", "scatter", "tab", "tabpe",
                                                "step")} for l in range(2)]

        bk = Banks(8)
        moe_base = []
        BX, BG, BH, BY, BR = 0, 1, 2, 3, 4
        NA = HEADS_B * NT

        def plan_norm(n):
            for t in range(NT):
                for half in range(2):
                    bk.add(("xt", n, t, half), (2 * t + half) % (6 if n % 2 else 8))

        def plan_out(l):
            for nb in range(2):
                for t in range(NT):
                    bk.add(("out", l, t, nb), (nb * 4 + t + (6, 0)[l]) % 8)

        def plan_moe(l):
            bk.add(("lgT", l), 6)
            bk.add(("lg", l), 7)
            bk.add(("pos", l), 7)
            bk.add(("tab", l), 6)
            moe_base.append(list(bk.uses))
            for b in (BX, BG, BH, BY, BR):
                bk.uses[b] += NE

        plan_norm(0)
        for name, first in (("xa", 0), ("ga", 4), ("q", 0)):
            for m in range(4):
                bk.add((name, m), first + m)
        for m in range(4):
            bk.add(("ra", m), 4 + m % 2)
            bk.add(("ix", m), 6 + m % 2)
        for name, first in (("k", 0), ("v", 4)):
            for m in range(4):
                bk.add((name, m), first + m)
        for n in range(NA + 2):
            if n < NA:
                bk.add(("S", n), n % 2)
            if 1 <= n <= NA:
                bk.add(("T", n - 1), 2 + (n - 1) % 2)
            if n >= 2:
                bk.add(("O", n - 2), 4 + n % 2)
        plan_out(0)
        plan_norm(1)
        plan_moe(0)
        plan_norm(2)
        for H in range(HEADS_C + 2):
            for k in range(4):
                if H < HEADS_C:
                    bk.add(("c", H, k), k)
                if k == 0 and H >= 2:
                    bk.add(("o", H - 2), 7)
                if k == 1 and H >= 2:
                    bk.add(("osum", H - 2), 6)
                if 1 <= H <= HEADS_C:
                    for L in (2 * k, 2 * k + 1):
                        bk.add(("lev", H - 1, L), 4 + L % 2)
                    if k == 1:
                        bk.add(("khT", H - 1), 6)
                    if k == 2:
                        bk.add(("dst", H - 1), 6)
        plan_out(1)
        plan_norm(3)
        plan_moe(1)

        def wait_full(eng, job):
            b, n = bk.jobs[job]
            eng.wait_ge(filled[b], n + 1)

        def wait_drained(eng, job):
            b, n = bk.jobs[job]
            eng.wait_ge(drained[b], n + 1)

        def drains(ins, job):
            ins.then_inc(drained[bk.jobs[job][0]], 1)

        def bank(job):
            return ps[bk.jobs[job][0]]

        rings = {"a": ring_a, "b": ring_b}

        loads = {key: 0 for key in ring_in}
        w0_in, w1_in, e_loads = [], [], []

        def place(lst, r, s):
            loads[(r, s)] += 1
            lst.append((r, s, loads[(r, s)]))

        for i in range(7):
            place(w0_in, "a", i % 3)
        for l in range(2):
            if l == 1:
                for i in range(HEADS_C):
                    place(w1_in, "a", i % 3)
                place(w1_in, "a", 2)
                place(w1_in, "a", 0)
            e_loads.append(dict(loads))
            for key in loads:
                loads[key] += NE // 2

        def wblock(r, s, n):
            return rings[r][:, s, :].rearrange("p (c n) -> p c n", c=n)

        def exp_ring(j):
            return "ba"[j]

        block = ctx.enter_context(nc.Block())

        @block.sync
        def _(sp):
            for t in range(NT):
                sp.dma_start(h[:, t, :], x[0, t * P:(t + 1) * P, :]).then_inc(x_in[t], 16)
            sp.dma_start(vec[:], cols).then_inc(vec_in, 16)

            def w0_load(i):
                r, s, _ = w0_in[i]
                src = ab_w_in[0][:, i * 512:(i + 1) * 512] if i < 5 else \
                    ab_w_out[0][:, (i - 5) * 512:(i - 4) * 512]
                sp.dma_start(wblock(r, s, NC), src.rearrange("(c p) n -> p c n", p=P)).then_inc(ring_in[(r, s)], 16)

            w0_load(0)
            w0_load(1)
            sp.wait_ge(diag_zero, 2)
            for dst, src in ((m0["wa"], rg_w_a), (m0["wx"], rg_w_x)):
                for par in range(2):
                    sp.dma_start(dst[64 * par:64 * par + 64, :, 64 * par:64 * par + 64],
                                 src[0, par::2].rearrange("n c d -> c n d")).then_inc(diag_in, 16)
            w0_load(2)
            sp.dma_start(m0["rtab"][0:HEADS_B, 255:639], bias_rev[:, 0:384]).then_inc(rtab_in, 16)
            sp.wait_ge(rtab_full, 2)
            sp.dma_start(bias_d, m0["rtab"][0:HEADS_B, :]).then_inc(rtab_out, 16)
            sp.wait_ge(rtab_out, 16)

            def strip(hd):
                if hd >= 2:
                    wait_drained(sp, ("S", 4 * (hd - 2) + 3))
                sp.dma_start(m0["strip"][:, hd % 2, :],
                             bass.AP(tensor=bias_d.tensor, offset=hd * 640, ap=[[1, P], [1, T]])
                             ).then_inc(strip_in[hd % 2], 16)

            strip(0)
            strip(1)
            sp.dma_start(rt[:].rearrange("p a b c -> p (a b c)"), router).then_inc(router_in, 16)
            last_of = [("xa", 3), ("ga", 3), ("q", 3), ("k", 3), ("v", 3)]
            for i in range(3, 7):
                wait_full(sp, last_of[i - 3])
                w0_load(i)
            for hd in range(2, HEADS_B):
                strip(hd)

            def expert_load(l, e, j, first):
                r = exp_ring(j)
                srcs = [w[l, bass.ds(e, 1)].rearrange("a (c p) n -> p (a c) n", p=P) for w in (w_gate, w_up, w_down)]
                for s, b in enumerate((BG, BG, BY)):
                    if not first:
                        sp.wait_ge(filled[b], e + (moe_base[l][b] - 1))
                    sp.dma_start(wblock(r, s, (NC, NC, FC)[s]), srcs[s]).then_inc(ring_in[(r, s)], 16)

            def moe_loads(l):
                if l == 0:
                    sp.wait_ge(ya_ready, 1)
                    wait_full(sp, ("O", NA - 1))
                expert_load(l, 0, 0, True)
                for nb in range(2):
                    wait_full(sp, ("out", l, NT - 1, nb))
                expert_load(l, 1, 1, True)
                with sp.Fori(0, NE // 2 - 1) as i:
                    expert_load(l, i * 2 + 2, 0, False)
                    expert_load(l, i * 2 + 3, 1, False)

            def more_loads(l):
                sp.wait_ge(flag_ready, l + 1)
                more = sp.value_load(flag[0:1, l:l + 1], min_val=0, max_val=1)
                o = ov[l]
                with sp.If(more > 0):
                    with sp.Fori(0, NE) as e:
                        srcs = [w[l, bass.ds(e, 1)].rearrange("a (c p) n -> p (a c) n", p=P)
                                for w in (w_gate, w_up, w_down)]
                        sp.wait_ge(o["pe"], e * (4 * (BLOCKS - 1)) + 1)
                        for s in range(3):
                            sp.dma_start(wblock("a", s, (NC, NC, FC)[s]), srcs[s]).then_inc(o["w"], 16)
                    sp.wait_ge(o["pe"], NE * 4 * (BLOCKS - 1) + 1)

            moe_loads(0)
            more_loads(0)
            sp.wait_ge(filled[BG], moe_base[0][BG] + NE)
            for i, (r, s, _) in enumerate(w1_in):
                if i == 1:
                    sp.wait_ge(yrow_in[NT - 1], 32)
                if i == 2:
                    sp.wait_ge(filled[BY], moe_base[0][BY] + NE)
                if 3 <= i < HEADS_C:
                    wait_full(sp, ("c", i - 3, 3))
                if i >= HEADS_C:
                    wait_full(sp, ("c", i - 3, 3))
                if i < HEADS_C:
                    sp.dma_start(rings[r][:, s, :], c_w_in[i]).then_inc(ring_in[(r, s)], 16)
                else:
                    nb = i - HEADS_C
                    sp.dma_start(wblock(r, s, NC), c_w_out[0][:, nb * 512:(nb + 1) * 512]
                                 .rearrange("(c p) n -> p c n", p=P)).then_inc(ring_in[(r, s)], 16)
            moe_loads(1)
            more_loads(1)
            for t in range(NT):
                sp.wait_ge(out_ready, t + 1)
                sp.dma_start(out[0, t * P:(t + 1) * P, :], xh[:, t, :]).then_inc(out_stored, 16)
            sp.wait_ge(out_stored, 16 * NT)

        @block.tensor
        def _(pe):
            def opens(job):
                b, n = bk.jobs[job]
                if n > 0:
                    pe.wait_ge(drained[b], n)
                return ps[b]

            def fills(ins, job):
                ins.then_inc(filled[bk.jobs[job][0]], 1)

            def turn_rows(n, tiles=range(NT)):
                for t in tiles:
                    pe.wait_ge(xh_ready, n * NT + t + 1)
                    for half in range(2):
                        job = ("xt", n, t, half)
                        dst = opens(job)
                        for c in range(4):
                            mm = nc.tensor.transpose(dst[:, c * P:(c + 1) * P],
                                                     xh[:, t, (half * 4 + c) * P:(half * 4 + c + 1) * P], ident[:])
                        fills(mm, job)

            def xT_ready(n, tiles=range(NT)):
                for t in tiles:
                    for half in range(2):
                        wait_drained(pe, ("xt", n, t, half))

            def out_part(l, block, y, t, nb, c):
                r, s, k = block
                job = ("out", l, t, nb)
                if c == 0:
                    pe.wait_ge(ring_in[(r, s)], 16 * k)
                    opens(job)
                mm = nc.tensor.matmul(bank(job)[:], y[:, c, t * P:(t + 1) * P], wblock(r, s, NC)[:, c, :],
                                      start=(c == 0), stop=(c == NC - 1))
                if c == NC - 1:
                    fills(mm, job)

            def out_proj(l, blocks, y, begun):
                for nb in range(2):
                    for t in range(NT):
                        for c in range(begun[t] if nb == 0 else 0, NC):
                            out_part(l, blocks[nb], y, t, nb, c)

            def proj0(i, name):
                r, s, k = w0_in[i]
                pe.wait_ge(ring_in[(r, s)], 16 * k)
                w = wblock(r, s, NC)
                for m in range(4):
                    job = (name, m)
                    dst = opens(job)
                    for c in range(NC):
                        if name == "v":
                            a, b = xT[:, c, m * P:(m + 1) * P], w[:, c, :]
                        else:
                            a, b = w[:, c, m * P:(m + 1) * P], xT[:, c, :]
                        mm = nc.tensor.matmul(dst[:], a, b, start=(c == 0), stop=(c == NC - 1))
                    fills(mm, job)

            def scores(n):
                hd, i = n // NT, n % NT
                if n == 0:
                    for m in range(4):
                        wait_drained(pe, ("q", m))
                        wait_drained(pe, ("k", m))
                lo = 64 * (hd % 2)
                dst = opens(("S", n))
                fills(nc.tensor.matmul(dst[:, 0:(i + 1) * P], m0["q"][lo:lo + 64, hd // 2, i * P:(i + 1) * P],
                                       m0["k"][lo:lo + 64, hd // 2, 0:(i + 1) * P], start=True, stop=True), ("S", n))

            def turn_probs(n):
                i = n % NT
                pe.wait_ge(prob_ready, n + 1)
                dst = opens(("T", n))
                for kt in range(i + 1):
                    mm = nc.tensor.transpose(dst[:, kt * P:(kt + 1) * P], m0["s"][:, n % 3, kt * P:(kt + 1) * P],
                                             ident[:])
                fills(mm, ("T", n))

            def values(n):
                hd, i = n // NT, n % NT
                if n == 0:
                    for m in range(4):
                        wait_drained(pe, ("v", m))
                wait_drained(pe, ("T", n))
                lo = 64 * (hd % 2)
                dst = opens(("O", n))
                for kt in range(i + 1):
                    mm = nc.tensor.matmul(dst[lo:lo + 64, 0:P], m0["v"][:, kt, hd * 64:(hd + 1) * 64],
                                          m0["pt"][:, n % 2, kt * P:(kt + 1) * P], start=(kt == 0), stop=(kt == i))
                fills(mm, ("O", n))

            pe.wait_ge(made, 1)
            turn_rows(0)
            xT_ready(0)
            proj0(0, "xa")
            proj0(1, "ga")
            proj0(2, "q")
            pe.wait_ge(diag_in, 64)
            for m in range(4):
                pe.wait_ge(xc_ready, m + 1)
                for name, w in (("ra", m0["wa"]), ("ix", m0["wx"])):
                    dst = opens((name, m))
                    fills(nc.tensor.matmul(dst[:], w[:, m, :], m0["xc"][:, m, :], start=True, stop=True), (name, m))
            proj0(3, "k")
            proj0(4, "v")
            scores(0)
            early = {4 + i: (i // 2, i % 2) for i in range(8)}
            for i in range(3):
                for t in range(2):
                    early[12 + 8 * i + t] = (4 + i, t)
            for n in range(NA + 2):
                if n + 1 < NA:
                    scores(n + 1)
                if 1 <= n <= NA:
                    turn_probs(n - 1)
                c, t = early.get(n, (None, None))
                if c == 0:
                    pe.wait_ge(ya_ready, 1)
                if c is not None:
                    if c >= 4:
                        for hd in range(2):
                            wait_drained(pe, ("O", (2 * (c - 4) + hd) * NT + t))
                    out_part(0, w0_in[5], m0["y"], t, 0, c)
                if n >= 2:
                    values(n - 2)
            for n in (NA - 2, NA - 1):
                wait_drained(pe, ("O", n))
            out_proj(0, w0_in[5:7], m0["y"], [7, 7, 0, 0])

            def pick_rows(l, e, j):
                pe.wait_ge(sel_ready, e + (l * NE + 1))
                pe.wait_ge(drained[BR], e + moe_base[l][BR])
                pe.sem_inc(turning, 1)
                for t in range(NT):
                    for z in range(2):
                        mm = nc.tensor.matmul(ps[BR][64 * z:64 * z + CAP, :], me["sel"][:, j, t * CAP:(t + 1) * CAP],
                                              xh[:, t, z * 512:(z + 1) * 512], start=(t == 0), stop=(t == NT - 1))
                mm.then_inc(filled[BR], 1)

            def turn_picked(l, e):
                pe.wait_ge(drained[BR], e + (moe_base[l][BR] + 1))
                pe.wait_ge(drained[BX], e + moe_base[l][BX])
                pe.sem_inc(turning, 1)
                for c in range(4):
                    mm = nc.tensor.transpose(ps[BX][:, c * P:(c + 1) * P], me["picked"][:, c * P:(c + 1) * P], ident[:])
                mm.then_inc(filled[BX], 1)

            def turn_in():
                for c in range(NC):
                    mm = nc.tensor.transpose(ps[BX][:, c * CAP:(c + 1) * CAP],
                                             me["rows"][0:CAP, 0, c * P:(c + 1) * P], ident[0:CAP, 0:CAP])
                return mm

            def gate_up(r, j):
                for c in range(NC):
                    for s in range(2):
                        mm = nc.tensor.matmul(ps[BG][64 * s:64 * s + CAP, :], me["xgT"][:, j, c * CAP:(c + 1) * CAP],
                                              wblock(r, s, NC)[:, c, :], start=(c == 0), stop=(c == NC - 1))
                return mm

            def turn_hidden():
                for c in range(FC):
                    mm = nc.tensor.transpose(ps[BH][:, c * CAP:(c + 1) * CAP], me["hrow"][0:CAP, c * P:(c + 1) * P],
                                             ident[0:CAP, 0:CAP])
                return mm

            def down(r):
                for c in range(FC):
                    for z in range(2):
                        mm = nc.tensor.matmul(ps[BY][64 * z:64 * z + CAP, :], me["hT"][:, c * CAP:(c + 1) * CAP],
                                              wblock(r, 2, FC)[:, c, z * 512:(z + 1) * 512],
                                              start=(c == 0), stop=(c == FC - 1))
                return mm

            def expert(l, e, k, j, ahead=2):
                base, r = moe_base[l], exp_ring(j)
                pe.wait_ge(drained[BX], e + (base[BX] + 1))
                for s in range(2):
                    pe.wait_ge(ring_in[(r, s)], k * 16 + 16 * (e_loads[l][(r, s)] + 1))
                pe.wait_ge(drained[BG], e + base[BG])
                gate_up(r, j).then_inc(filled[BG], 1)
                if isinstance(e, int) and e == 0:
                    pick_rows(l, 1, 1)
                if ahead >= 1:
                    turn_picked(l, e + 1)
                pe.wait_ge(drained[BG], e + (base[BG] + 1))
                pe.wait_ge(drained[BH], e + base[BH])
                pe.sem_inc(turning, 1)
                turn_hidden().then_inc(filled[BH], 1)
                if ahead >= 2:
                    pick_rows(l, e + 2, j)
                pe.wait_ge(ring_in[(r, 2)], k * 16 + 16 * (e_loads[l][(r, 2)] + 1))
                pe.wait_ge(drained[BH], e + (base[BH] + 1))
                pe.wait_ge(drained[BY], e + base[BY])
                down(r).then_inc(filled[BY], 1)

            def more_blocks(l):
                pe.wait_ge(flag_ready, l + 1)
                more = pe.value_load(flag[0:1, l:l + 1], min_val=0, max_val=1)
                o, per_e = ov[l], BLOCKS - 1
                with pe.If(more > 0):
                    pe.wait_ge(drained[BY], moe_base[l][BY] + NE)
                    pe.sem_inc(o["pe"], 1)
                    with pe.Fori(0, per_e) as b:
                        pe.wait_ge(o["tab"], b * 2 + 1)
                        for i in range(2 * NT):
                            mm = nc.tensor.matmul(ps[6][0:CAP, 0:NE], me["A"][:, i // NT, i % NT, :],
                                                  me["B"][:, i // NT, i % NT, :], start=(i == 0), stop=(i == 2 * NT - 1))
                        mm.then_inc(o["tabpe"], 1)
                    with pe.Fori(0, NE) as e:
                        with pe.Fori(0, per_e) as b:
                            n = e * per_e + b
                            pe.wait_ge(o["w"], e * 48 + 48)
                            pe.wait_ge(o["gather"], n * 16 + 16)
                            pe.sem_inc(turning, 1)
                            turn_in().then_inc(o["pe"], 1)
                            pe.wait_ge(o["dve"], n * 4 + 1)
                            gate_up("a", 0).then_inc(o["pe"], 1)
                            pe.wait_ge(o["dve"], n * 4 + 2)
                            pe.sem_inc(turning, 1)
                            turn_hidden().then_inc(o["pe"], 1)
                            pe.wait_ge(o["dve"], n * 4 + 3)
                            down("a").then_inc(o["pe"], 1)

            def moe(l):
                n = 2 * l + 1
                turn_rows(n, range(2))
                pe.wait_ge(router_in, 16)
                dst = opens(("lgT", l))
                for t in range(NT):
                    if t + 2 < NT:
                        turn_rows(n, [t + 2])
                    xT_ready(n, [t])
                    for c in range(NC):
                        mm = nc.tensor.matmul(dst[0:NG + NE, t * P:(t + 1) * P], rt[:, l, c, :],
                                              xT[:, c, t * P:(t + 1) * P], start=(c == 0), stop=(c == NC - 1))
                fills(mm, ("lgT", l))
                wait_drained(pe, ("lgT", l))
                dst = opens(("lg", l))
                for t in range(NT):
                    mm = nc.tensor.transpose(dst[:, t * 64:t * 64 + NG + NE], me["lgT"][0:NG + NE, t * P:(t + 1) * P],
                                             ident[0:NG + NE, 0:NG + NE])
                fills(mm, ("lg", l))
                pe.wait_ge(one_hot, l + 1)
                dst = opens(("pos", l))
                nc.tensor.matmul(dst[:, 0:NT * NE], tri[:], me["M"].rearrange("p t n -> p (t n)"),
                                 start=True, stop=False)
                nc.tensor.matmul(dst[:, NE:NT * NE], ones[:], me["Msum"][:, 0:NT - 1, :].rearrange("p t n -> p (t n)"),
                                 start=False, stop=True)
                mm = nc.tensor.matmul(dst[:, 256:256 + NE], ones[:], me["Msum"][:, NT - 1, :], start=True, stop=True)
                fills(mm, ("pos", l))
                pick_rows(l, 0, 0)
                turn_picked(l, 0)
                pe.wait_ge(slots_hot, l + 1)
                dst = opens(("tab", l))
                for i in range(2 * NT):
                    mm = nc.tensor.matmul(dst[0:CAP, 0:NE], me["A"][:, i // NT, i % NT, :],
                                          me["B"][:, i // NT, i % NT, :], start=(i == 0), stop=(i == 2 * NT - 1))
                fills(mm, ("tab", l))
                expert(l, 0, 0, 0)
                with pe.Fori(0, NE // 2 - 2) as i:
                    expert(l, i * 2 + 1, i, 1)
                    expert(l, i * 2 + 2, i + 1, 0)
                expert(l, NE - 3, NE // 2 - 2, 1)
                expert(l, NE - 2, NE // 2 - 1, 0, ahead=1)
                expert(l, NE - 1, NE // 2 - 1, 1, ahead=0)
                more_blocks(l)

            moe(0)

            def proj1(H, k):
                r, s, n = w1_in[H]
                if k == 0:
                    pe.wait_ge(ring_in[(r, s)], 16 * n)
                w = rings[r][:, s, :].rearrange("p (c k n) -> p c k n", c=NC, k=4)
                dst = opens(("c", H, k))
                if k == 2:
                    for t in range(NT):
                        for c in range(NC):
                            mm = nc.tensor.matmul(dst[:, t * P:(t + 1) * P], xT[:, c, t * P:(t + 1) * P], w[:, c, k, :],
                                                  start=(c == 0), stop=(c == NC - 1))
                else:
                    for c in range(NC):
                        mm = nc.tensor.matmul(dst[:], w[:, c, k, :], xT[:, c, :], start=(c == 0), stop=(c == NC - 1))
                fills(mm, ("c", H, k))

            def level(H, L):
                if L == 0:
                    wait_drained(pe, ("c", H, 1))
                    pe.wait_ge(kk_ready, H + 1)
                    a, b = m1["kk"][:, H % 2, :], m1["q"][:, H % 2, :]
                else:
                    pe.wait_ge(qk_ready, H * LEVELS + L)
                    a = b = m1["qk"][:, L % 2, :]
                dst = opens(("lev", H, L))
                for j in range(NT):
                    sl = slice(j * P, (j + 1) * P)
                    mm = nc.tensor.matmul(dst[:, sl], a[:, sl], b[:, sl], start=True, stop=True)
                fills(mm, ("lev", H, L))

            def turn_keys(H):
                pe.wait_ge(kh_ready, H + 1)
                dst = opens(("khT", H))
                for j in range(NT - 1):
                    mm = nc.tensor.transpose(dst[:, j * P:(j + 1) * P], m1["dl"][:, j, :], ident[:])
                fills(mm, ("khT", H))

            def chunk_states(H):
                wait_drained(pe, ("khT", H))
                wait_drained(pe, ("c", H, 2))
                dst = opens(("dst", H))
                for j in range(NT - 1):
                    sl = slice(j * P, (j + 1) * P)
                    mm = nc.tensor.matmul(dst[:, sl], m1["kh"][:, j, :], m1["v"][:, H % 2, sl], start=True, stop=True)
                fills(mm, ("dst", H))

            def head_out(H):
                wait_drained(pe, ("lev", H, LEVELS))
                wait_drained(pe, ("dst", H))
                pe.wait_ge(qe_ready, H + 1)
                dst = opens(("o", H))
                for j in range(NT):
                    sl = slice(j * P, (j + 1) * P)
                    mm = nc.tensor.matmul(dst[:, sl], m1["v"][:, H % 2, sl], m1["attn"][:, H % 2, sl],
                                          start=True, stop=(j == 0))
                    if j > 0:
                        mm = nc.tensor.matmul(dst[:, sl], m1["st"][:, H % 2, (j - 1) * P:j * P], m1["qe"][:, H % 2, sl],
                                              start=False, stop=True)
                fills(mm, ("o", H))

            def head_sum(H):
                pe.wait_ge(osq_ready, H + 1)
                dst = opens(("osum", H))
                fills(nc.tensor.matmul(dst[:], ones[:], m1["sq"][:], start=True, stop=True), ("osum", H))

            turn_rows(2)
            xT_ready(2)
            for H in range(HEADS_C + 2):
                for k in range(4):
                    if H < HEADS_C:
                        proj1(H, k)
                    if k == 0 and H >= 2:
                        head_out(H - 2)
                    if k == 1 and H >= 2:
                        head_sum(H - 2)
                    if H == HEADS_C:
                        pe.wait_ge(y_ready, HEADS_C - 2)
                        for c in range(HEADS_C - 2):
                            out_part(1, w1_in[8], m1["y"], k, 0, c)
                    if 1 <= H <= HEADS_C:
                        level(H - 1, 2 * k)
                        level(H - 1, 2 * k + 1)
                        if k == 1:
                            turn_keys(H - 1)
                        if k == 2:
                            chunk_states(H - 1)
            pe.wait_ge(y_ready, HEADS_C)
            out_proj(1, w1_in[8:10], m1["y"], [HEADS_C - 2] * NT)
            moe(1)

        @block.scalar
        def _(act):
            A = nc.scalar.activation

            def norm(n):
                squares = [xh[:, t, :] for t in range(NT)] if n != 3 else [me["fin_g"]] * NT
                if n > 0:
                    A(warm[:], eps_t[:], ACT.Sqrt).then_inc(act_step, 1)
                for t in range(NT):
                    if n == 0:
                        act.wait_ge(x_in[t], 16)
                    elif n % 2 == 1:
                        for nb in range(2):
                            wait_drained(act, ("out", n // 2, t, nb))
                    else:
                        act.wait_ge(h_ready, (n // 2 - 1) * 2 * NT + 2 * t + 2)
                    if n == 0 and t == 0:
                        act.wait_ge(eps_made, 1)
                    if n == 3 and t > 0:
                        act.wait_ge(ss_ready, n * NT + t)
                    A(squares[t], h[:, t, :], ACT.Square, accum_out=ss[:, n, t:t + 1]).then_inc(ss_ready, 1)
                    act.wait_ge(ss_ready, n * NT + t + 1)
                    A(std[:, n, t:t + 1], ss[:, n, t:t + 1], ACT.Sqrt, bias=eps_t[:, 0:1], scale=1.0 / D
                      ).then_inc(std_ready, 1)

            norm(0)
            act.wait_ge(lam_in, 1)
            A(lamt[:, 1, :], lamt[:, 0, :], ACT.Exp, scale=-1.0).then_inc(lam_exp, 1)
            act.wait_ge(lb_in, 2)
            A(lbt[:, 2:4, :], lbt[:, 0:2, :], ACT.Exp).then_inc(lb_exp, 1)

            for m in range(4):
                wait_full(act, ("xa", m))
                drains(A(m0["xa"][:, m, 3:3 + T], bank(("xa", m))[:], ACT.Copy), ("xa", m))
            for m in range(4):
                wait_full(act, ("ga", m))
                drains(A(m0["ga"][:, m, :], bank(("ga", m))[:], ACT.Copy), ("ga", m))
            for m in range(4):
                for name, dst, b in (("ra", "r", "b_a"), ("ix", "i", "b_x")):
                    wait_full(act, (name, m))
                    drains(A(m0[dst][:, m, :], bank((name, m))[:], ACT.Sigmoid, bias=at[b][:, m:m + 1]), (name, m))
            act.wait_ge(cl_ready, 2)
            for m in range(4):
                wait_drained(act, ("ra", m))
                A(m0["a"][:, m, :], m0["r"][:, m, :], ACT.Exp, scale=cl[:, 0, m:m + 1]).then_inc(rg_a, 1)
            act.wait_ge(rg_a, 4)
            for m in range(4):
                A(m0["r"][:, m, :], m0["r"][:, m, :], ACT.Tanh, scale=cl[:, 1, m:m + 1]).then_inc(rg_t, 1)
            act.wait_ge(gelu_in, 1)
            A(m0["xa"][:, :, 0:T], m0["xa"][:, :, 0:T], ACT.Tanh, scale=GELU_B).then_inc(gelu_t, 1)
            for m in range(4):
                wait_full(act, ("k", m))
                drains(A(m0["k"][:, m, :], bank(("k", m))[:], ACT.Copy), ("k", m))
            act.wait_ge(rg_m2, 1)
            A(m0["xc"], m0["xc"], ACT.Sqrt).then_inc(rg_m, 1)
            for m in range(4):
                wait_full(act, ("v", m))
                drains(A(m0["v"][:, m, :], bank(("v", m))[:], ACT.Copy), ("v", m))
            for n in range(NA + 1):
                if n < NA:
                    N = (n % NT + 1) * P
                    act.wait_ge(score_max, n + 1)
                    A(m0["s"][:, n % 3, 0:N], m0["s"][:, n % 3, 0:N], ACT.Exp, bias=m0["nmx"][:, n:n + 1],
                      accum_out=m0["sum"][:, n:n + 1]).then_inc(prob_exp, 1)
                if n >= 1:
                    q = n - 1
                    N = (q % NT + 1) * P
                    wait_full(act, ("T", q))
                    if q >= 2:
                        wait_full(act, ("O", q - 2))
                    drains(A(m0["pt"][:, q % 2, 0:N], bank(("T", q))[:, 0:N], ACT.Copy), ("T", q))

            def picked(l, e):
                base = moe_base[l]
                act.wait_ge(filled[BR], e + (base[BR] + 1))
                if not (isinstance(e, int) and e == 0):
                    act.wait_ge(filled[BX], e + base[BX])
                A(me["picked"], ps[BR][:], ACT.Copy).then_inc(drained[BR], 1)

            def act_expert(l, e, k, j, ahead=True):
                base = moe_base[l]
                act.wait_ge(filled[BG], e + (base[BG] + 1))
                if not (isinstance(e, int) and e < 2):
                    act.wait_ge(drained[BG], e + (base[BG] - 1))
                A(me["silu"][64:128, j, :], ps[BG][0:CAP, :], ACT.Silu).then_inc(silu_ready, 1)
                if isinstance(e, int) and e == 0:
                    picked(l, 1)
                if ahead:
                    picked(l, e + 2)
                act.wait_ge(filled[BY], e + (base[BY] + 1))
                if not (isinstance(k, int) and k == 0):
                    act.wait_ge(scattered[j], k * 16 + 16 * l * (NE // 2))
                A(me["rows"][0:CAP, 2 + j, 0:512], ps[BY][0:CAP, :], ACT.Copy).then_inc(half_out, 1)

            def more_blocks(l):
                act.wait_ge(flag_ready, l + 1)
                more = act.value_load(flag[0:1, l:l + 1], min_val=0, max_val=1)
                o = ov[l]
                with act.If(more > 0):
                    for t in range(NT):
                        act.dma_start(xg_d[l][t * P:(t + 1) * P, :], xh[:, t, :]).then_inc(xh_stored[l], 16)
                    with act.Fori(0, NE * (BLOCKS - 1)) as n:
                        act.wait_ge(o["pe"], n * 4 + 3)
                        A(me["silu"][64:128, 0, :], ps[BG][0:CAP, :], ACT.Silu).then_inc(o["act"], 1)
                        act.wait_ge(o["pe"], n * 4 + 5)
                        A(me["rows"][0:CAP, 2, 0:512], ps[BY][0:CAP, :], ACT.Copy).then_inc(o["act"], 1)

            def moe(l):
                norm(2 * l + 1)
                act.wait_ge(route_in, l + 1)
                A(me["ex"], me["ex"], ACT.Exp).then_inc(route_exp, 1)
                picked(l, 0)
                act_expert(l, 0, 0, 0)
                act_expert(l, 1, 0, 1)
                with act.Fori(1, NE // 2 - 1) as i:
                    act_expert(l, i * 2, i, 0)
                    act_expert(l, i * 2 + 1, i, 1)
                act_expert(l, NE - 2, NE // 2 - 1, 0, ahead=False)
                act_expert(l, NE - 1, NE // 2 - 1, 1, ahead=False)
                more_blocks(l)
                if l == 1:
                    act.dma_start(me["fin_g"], final_g[None, :].broadcast_to([P, D])).then_inc(final_in, 16)
                for j in range(2):
                    act.wait_ge(scattered[j], 16 * (l + 1) * (NE // 2))
                act.wait_ge(ov_done, l + 1)
                for t in range(NT):
                    for k in range(2):
                        act.dma_start(yrows[:, 2 * t + k, :], y_d[l][k * T + t * P:k * T + (t + 1) * P, :]
                                      ).then_inc(yrow_in[t], 16)

            moe(0)
            norm(2)

            def exp_level(G, L):
                act.wait_ge(e_sub, G * LEVELS + L)
                A(m1["e"][:, L % 2, :], m1["e"][:, L % 2, :], ACT.Exp).then_inc(e_exp, 1)

            for H in range(HEADS_C + 2):
                new, G, O = H < HEADS_C, H - 1, H - 2
                core, outp = 0 <= G < HEADS_C, O >= 0
                if core:
                    exp_level(G, 1)
                    exp_level(G, 2)
                    act.wait_ge(b_ready, G + 1)
                    if G > 0:
                        act.wait_ge(qe_ready, G)
                        wait_drained(act, ("dst", G - 1))
                    A(m1["eb"], m1["b"][:, G % 2, :], ACT.Exp).then_inc(eb_ready, 1)
                    act.wait_ge(dl_sub, G + 1)
                    A(m1["dl"], m1["dl"], ACT.Exp).then_inc(dl_exp, 1)
                if new:
                    wait_full(act, ("c", H, 0))
                    if H > 0:
                        act.wait_ge(kk_ready, H)
                        act.wait_ge(lf_ready, H)
                    drains(A(m1["f"], bank(("c", H, 0))[:], ACT.Sigmoid), ("c", H, 0))
                if outp:
                    wait_full(act, ("o", O))
                    if O > 0:
                        wait_full(act, ("osum", O - 1))
                    A(m1["sq"], bank(("o", O))[:], ACT.Square).then_inc(osq_ready, 1)
                if core:
                    exp_level(G, 3)
                    exp_level(G, 4)
                if new:
                    act.wait_ge(f_ready, H + 1)
                    if H > 2:
                        act.wait_ge(y_ready, H - 2)
                    A(m1["b"][:, H % 2, :], m1["f"], ACT.Ln).then_inc(lf_ready, 1)
                if outp:
                    wait_full(act, ("osum", O))
                    if O > 0:
                        act.wait_ge(y_ready, O)
                    drains(A(m1["rs"], bank(("osum", O))[:], ACT.Ln, bias=eps_t[:, 0:1], scale=1.0 / P), ("osum", O))
                    wait_drained(act, ("osum", O))
                    A(m1["rs"], m1["rs"], ACT.Exp, scale=-0.5).then_inc(rs_ready, 1)
                if core:
                    wait_full(act, ("khT", G))
                    if G > 0:
                        wait_full(act, ("dst", G - 1))
                    drains(A(m1["kh"].rearrange("p a b -> p (a b)"), bank(("khT", G))[:, 0:3 * P], ACT.Copy), ("khT", G))
                    exp_level(G, 5)
                    exp_level(G, 6)
                if new:
                    wait_full(act, ("c", H, 2))
                    drains(A(m1["v"][:, H % 2, :], bank(("c", H, 2))[:], ACT.Copy), ("c", H, 2))
                if core:
                    exp_level(G, 7)
                if new:
                    wait_full(act, ("c", H, 1))
                    if H >= 2:
                        act.wait_ge(qk_ready, (H - 1) * LEVELS)
                        act.wait_ge(qe_ready, H - 1)
                        act.wait_ge(y_ready, H - 1)
                    drains(A(m1["q"][:, H % 2, :], bank(("c", H, 1))[:], ACT.Silu), ("c", H, 1))
                    wait_full(act, ("c", H, 3))
                    drains(A(m1["sg"][:, H % 2, :], bank(("c", H, 3))[:], ACT.Silu), ("c", H, 3))
            moe(1)
            norm(4)

        @block.gpsimd
        def _(pool):
            g = nc.gpsimd
            st = Steps(pool, pool_step)
            g.memset(eps_t[:], EPS).then_inc(eps_made, 1)
            st.then(g.memset(ident[:], 0.0))
            g.affine_select(out=ident[:], in_=ident[:], compare_op=ALU.not_equal, fill=1.0, base=0,
                            pattern=[[-1, P]], channel_multiplier=1).then_inc(made, 1)
            g.memset(m0["wa"], 0.0).then_inc(diag_zero, 1)
            g.memset(m0["wx"], 0.0).then_inc(diag_zero, 1)

            st.then(g.memset(ones[:], 1.0))
            g.affine_select(out=tri[:], in_=ones[:], compare_op=ALU.is_gt, fill=0.0, base=0,
                            pattern=[[1, P]], channel_multiplier=-1).then_inc(made, 1)
            g.iota(iota[:], [[1, CAP]], base=0, channel_multiplier=0, allow_small_or_imprecise_dtypes=True
                   ).then_inc(made, 1)
            g.iota(gkey[:], [[-1, NG]], base=NG, channel_multiplier=0, allow_small_or_imprecise_dtypes=True
                   ).then_inc(made, 1)
            g.iota(ekey[:], [[-1, NE]], base=NE, channel_multiplier=0, allow_small_or_imprecise_dtypes=True
                   ).then_inc(made, 1)
            g.iota(tokval[:], [[T, 2], [P, NT]], base=1, channel_multiplier=1,
                   allow_small_or_imprecise_dtypes=True).then_inc(made, 1)
            st.then(g.memset(keep[:], 1.0))
            g.memset(keep[:].rearrange("p (a b) -> p a b", a=NT)[:, :, 0:1], 0.0).then_inc(made, 1)
            for L in range(1, LEVELS + 1):
                m = P >> L
                nb = P // (2 * m)
                v = masks[:, L - 1, :].rearrange("p (a b) -> p a b", a=nb)
                st.then(g.memset(masks[:, L - 1, :], 0.0))
                w = v[:, :, m:2 * m]
                st.then(g.memset(w, 1.0))
                st.then(g.affine_select(out=w, in_=w, compare_op=ALU.is_ge, fill=0.0, base=0,
                                        pattern=[[-2 * m, nb], [0, m]], channel_multiplier=1))
                ins = g.affine_select(out=w, in_=w, compare_op=ALU.is_gt, fill=0.0, base=m,
                                      pattern=[[2 * m, nb], [0, m]], channel_multiplier=-1)
                if L < LEVELS:
                    st.then(ins)
                else:
                    ins.then_inc(made, 1)

            def scatter_rows(l, j):
                pool.sem_inc(moving, 1)
                g.indirect_dma_start(out=y_d[l], out_offset=bass.IndirectOffsetOnAxis(ap=si[j][:, 0:1], axis=0),
                                     in_=me["rows"][0:CAP, 2 + j, :], in_offset=None,
                                     bounds_check=2 * T - 1, oob_is_err=False).then_inc(scattered[j], 16)

            def moe(l):
                base = moe_base[l]
                for n in (0, 1):
                    wait_full(pool, ("out", l, NT - 1, n))
                g.memset(me["rows"][0:CAP, 0, :], 0.0).then_inc(pool_rows, 1)
                pool.wait_ge(table_ready, l + 1)

                def slots_of(e, j):
                    g.tensor_copy(me["slot"][:, j, :], me["slots"][:, :, bass.ds(e, 1)].rearrange("p t a -> p (t a)")
                                  ).then_inc(col_ready, 1)

                def step(e, k, j, ahead=True):
                    if ahead:
                        pool.wait_ge(sel_ready, e + (l * NE + 1))
                        slots_of(e + 2, j)
                    if not (isinstance(k, int) and k == 0):
                        pool.wait_ge(scattered[j], k * 16 + 16 * (l * (NE // 2)))
                    elif l > 0:
                        pool.wait_ge(scattered[j], 16 * l * (NE // 2))
                    g.tensor_copy(si[j][:], ri[:, bass.ds(e, 1)]).then_inc(idx_copied, 1)
                    pool.wait_ge(idx_copied, e + (l * NE + 1))
                    pool.wait_ge(drained[BY], e + (base[BY] + 1))
                    scatter_rows(l, j)

                step(0, 0, 0)
                step(1, 0, 1)
                with pool.Fori(1, NE // 2 - 1) as i:
                    step(i * 2, i, 0)
                    step(i * 2 + 1, i, 1)
                step(NE - 2, NE // 2 - 1, 0, ahead=False)
                step(NE - 1, NE // 2 - 1, 1, ahead=False)
                for j in range(2):
                    pool.wait_ge(scattered[j], 16 * (l + 1) * (NE // 2))
                more_blocks(l)
                pool.sem_inc(ov_done, 1)

            def more_blocks(l):
                pool.wait_ge(flag_ready, l + 1)
                more = pool.value_load(flag[0:1, l:l + 1], min_val=0, max_val=1)
                o, per_e = ov[l], BLOCKS - 1
                with pool.If(more > 0):
                    pool.wait_ge(o["pe"], 1)
                    pool.wait_ge(o["tab"], 2 * per_e)
                    pool.wait_ge(pool_rows, l + 1)
                    pool.wait_ge(xh_stored[l], 16 * NT)
                    with pool.Fori(0, NE) as e:
                        with pool.Fori(0, per_e) as b:
                            n = e * per_e + b
                            col = b * NE + e
                            g.tensor_copy(gi[:], xio[:, bass.ds(col, 1)]).then_inc(o["idx"], 1)
                            g.tensor_copy(si[0][:], rio[:, bass.ds(col, 1)]).then_inc(o["idx"], 1)
                            pool.wait_ge(o["idx"], n * 2 + 2)
                            pool.sem_inc(moving, 1)
                            g.indirect_dma_start(out=me["rows"][0:CAP, 0, :], out_offset=None, in_=xg_d[l],
                                                 in_offset=bass.IndirectOffsetOnAxis(ap=gi[:, 0:1], axis=0),
                                                 bounds_check=T - 1, oob_is_err=False).then_inc(o["gather"], 16)
                            pool.wait_ge(o["dve"], n * 4 + 4)
                            pool.sem_inc(moving, 1)
                            g.indirect_dma_start(out=y_d[l],
                                                 out_offset=bass.IndirectOffsetOnAxis(ap=si[0][:, 0:1], axis=0),
                                                 in_=me["rows"][0:CAP, 2, :], in_offset=None,
                                                 bounds_check=2 * T - 1, oob_is_err=False).then_inc(o["scatter"], 16)
                            pool.wait_ge(o["scatter"], n * 16 + 16)
                            pool.sem_inc(moving, 1)

            moe(0)

            def mix_level(G, L):
                m = P >> L
                nb = T // (2 * m)
                view = lambda t: t.rearrange("p (a b) -> p a b", a=nb)
                e, qk = view(m1["e"][:, L % 2, :]), view(m1["qk"][:, L % 2, :])
                q, kk = view(m1["q"][:, G % 2, :]), view(m1["kk"][:, G % 2, :])
                pool.wait_ge(e_exp, G * LEVELS + L)
                if L == 1:
                    wait_drained(pool, ("c", G, 1))
                    pool.wait_ge(kk_ready, G + 1)
                if L >= 3:
                    wait_full(pool, ("lev", G, L - 2))
                elif G > 0:
                    wait_full(pool, ("lev", G - 1, L + 4 if L == 2 else 7))
                g.tensor_tensor(qk[:, :, 0:m], kk[:, :, 0:m], e[:, :, 0:m], ALU.mult)
                g.tensor_tensor(qk[:, :, m:2 * m], q[:, :, m:2 * m], e[:, :, m:2 * m], ALU.mult
                                ).then_inc(qk_ready, 1)

            for H in range(HEADS_C + 1):
                new, G = H < HEADS_C, H - 1
                core = G >= 0
                if core:
                    mix_level(G, 1)
                    mix_level(G, 2)
                    pool.wait_ge(dl_exp, G + 1)
                    g.tensor_tensor(m1["dl"], m1["dl"],
                                    m1["kk"][:, G % 2, 0:3 * P].rearrange("p (a b) -> p a b", a=3), ALU.mult
                                    ).then_inc(kh_ready, 1)
                if new:
                    pool.wait_ge(f_ready, H + 1)
                    if H >= 2:
                        wait_full(pool, ("lev", H - 2, 0))
                    g.tensor_scalar(m1["kk"][:, H % 2, :], m1["f"], -1.0, 1.0, ALU.mult, ALU.add).then_inc(kk_ready, 1)
                if core:
                    for L in (3, 4):
                        mix_level(G, L)
                    pool.wait_ge(eb_ready, G + 1)
                    if G >= 2:
                        wait_full(pool, ("o", G - 2))
                    g.tensor_tensor(m1["qe"][:, G % 2, :], m1["q"][:, G % 2, :], m1["eb"], ALU.mult
                                    ).then_inc(qe_ready, 1)
                    for L in (5, 6, 7):
                        mix_level(G, L)
                if new:
                    wait_drained(pool, ("c", H, 3))
                    g.tensor_scalar(m1["sg"][:, H % 2, :], m1["sg"][:, H % 2, :], at["norm_g"][:, H:H + 1], None,
                                    ALU.mult).then_inc(sgg_ready, 1)
            moe(1)

        @block.vector
        def _(dve):
            v = nc.vector
            st = Steps(dve, dve_step)

            def norm_col(n, t):
                dve.wait_ge(std_ready, n * NT + t + 1)
                v.reciprocal(rstd[:, n, t:t + 1], std[:, n, t:t + 1]).then_inc(rstd_ready, 1)

            def norm_rows(n, t):
                if n == 3 and t == 0:
                    wait_full(dve, ("out", 1, NT - 1, 1))
                dve.wait_ge(rstd_ready, n * NT + t + 1)
                v.tensor_scalar(xh[:, t, :], h[:, t, :], rstd[:, n, t:t + 1], None, ALU.mult).then_inc(xh_ready, 1)

            def turned_rows(n, t):
                gain = at["mix_g" if n % 2 == 0 else "ffn_g"]
                for half in range(2):
                    job = ("xt", n, t, half)
                    c0 = (n // 2) * NC + half * 4
                    wait_full(dve, job)
                    drains(v.tensor_tensor(xT[:, half * 4:half * 4 + 4, t * P:(t + 1) * P],
                                           bank(job)[:].rearrange("p (c t) -> p c t", c=4),
                                           gain[:, c0:c0 + 4].unsqueeze(2).broadcast_to([P, 4, P]), ALU.mult), job)

            def add_out(l, nb, t):
                job = ("out", l, t, nb)
                wait_full(dve, job)
                hh = h[:, t, nb * 512:(nb + 1) * 512]
                drains(v.tensor_tensor(hh, bank(job)[:], hh, ALU.add), job)

            def mixer_end(l):
                n = 2 * l + 1
                for t in range(NT):
                    add_out(l, 0, t)
                for t in range(NT):
                    add_out(l, 1, t)
                    if t < NT - 1:
                        norm_col(n, t)
                        if l == 0:
                            norm_rows(n, t)
                if l == 1:
                    for t in range(NT - 1):
                        norm_rows(n, t)
                norm_col(n, NT - 1)
                norm_rows(n, NT - 1)
                for t in range(NT):
                    turned_rows(n, t)

            v.memset(m0["rtab"][0:HEADS_B, 639:640], 0.0).then_inc(rtab_full, 1)
            dve.wait_ge(vec_in, 16)
            for t in range(NT + 1):
                if t < NT:
                    norm_col(0, t)
                    norm_rows(0, t)
                if t > 0:
                    turned_rows(0, t - 1)
            v.memset(m0["xa"][:, :, 0:3], 0.0).then_inc(dve_made, 1)
            dve.wait_ge(rtab_in, 16)
            v.tensor_copy(m0["rtab"][0:HEADS_B, 0:255], m0["rtab"][0:HEADS_B, 255:256].broadcast_to([HEADS_B, 255])
                          ).then_inc(rtab_full, 1)
            lam, u, w, acc = at["lam"], lamt[:, 1, :], lamt[:, 2, :], lamt[:, 3, :]
            v.scalar_tensor_tensor(out=lamt[:, 0, :], in0=lam, scalar=-1.0, in1=lam, op0=ALU.mult, op1=ALU.max
                                   ).then_inc(lam_in, 1)
            st.then(v.tensor_tensor(lb[:], at["lb0"], at["lb1"], ALU.max))
            v.tensor_tensor(lbt[:, 0, :], at["lb0"], lb[:], ALU.subtract).then_inc(lb_in, 1)
            v.tensor_tensor(lbt[:, 1, :], at["lb1"], lb[:], ALU.subtract).then_inc(lb_in, 1)
            dve.wait_ge(lam_exp, 1)
            st.then(v.tensor_scalar(w, u, 2.0, None, ALU.add))
            st.then(v.reciprocal(w, w))
            st.then(v.tensor_tensor(u, u, w, ALU.mult))
            st.then(v.tensor_tensor(w, u, u, ALU.mult))
            st.then(v.tensor_scalar(acc, w, 1.0 / 17, 1.0 / 15, ALU.mult, ALU.add))
            for k in (13, 11, 9, 7, 5, 3, 1):
                st.then(v.tensor_tensor(acc, acc, w, ALU.mult))
                st.then(v.tensor_scalar(acc, acc, 1.0 / k, None, ALU.add))
            st.then(v.tensor_tensor(acc, acc, u, ALU.mult))
            st.then(v.tensor_scalar(w, lam, 0.0, 0.5, ALU.min, ALU.mult))
            st.then(v.tensor_tensor(acc, w, acc, ALU.subtract))
            v.tensor_scalar(cl[:, 0, :], acc, 16.0, None, ALU.mult).then_inc(cl_ready, 1)
            v.tensor_scalar(cl[:, 1, :], acc, -16.0, None, ALU.mult).then_inc(cl_ready, 1)

            dve.wait_ge(dve_made, 1)
            for m in range(4):
                wait_drained(dve, ("xa", m))
                xc = m0["xc"][:, m, :]
                taps = [at["conv_w"][:, 4 * m + j:4 * m + j + 1] for j in range(CONV)]
                st.then(v.tensor_scalar(xc, m0["xa"][:, m, 0:T], taps[0], at["conv_b"][:, m:m + 1], ALU.mult, ALU.add))
                for j in (1, 2, 3):
                    ins = v.scalar_tensor_tensor(out=xc, in0=m0["xa"][:, m, j:j + T], scalar=taps[j], in1=xc,
                                                 op0=ALU.mult, op1=ALU.add)
                    if j < 3:
                        st.then(ins)
                    else:
                        ins.then_inc(xc_ready, 1)
            dve.wait_ge(xc_ready, 4)
            ga, gx = m0["ga"], m0["xa"][:, :, 0:T]
            for m in range(4):
                wait_drained(dve, ("ga", m))
            st.then(v.tensor_tensor(gx, ga, ga, ALU.mult))
            st.then(v.tensor_scalar(gx, gx, GELU_A, 1.0, ALU.mult, ALU.add))
            v.tensor_tensor(gx, gx, ga, ALU.mult).then_inc(gelu_in, 1)
            for m in range(4):
                job = ("q", m)
                wait_full(dve, job)
                drains(v.tensor_scalar(m0["q"][:, m, :].rearrange("p (i t) -> p i t", i=NT)[:, :, ::-1],
                                       bank(job)[:].rearrange("p (i t) -> p i t", i=NT), 0.125, None, ALU.mult), job)
            for m in range(4):
                wait_drained(dve, ("ix", m))
                wait_drained(dve, ("ra", m))
            v.tensor_tensor(m0["i"], m0["i"], m0["xc"], ALU.mult).then_inc(rg_x, 1)
            dve.wait_ge(rg_a, 4)
            dve.wait_ge(rg_x, 1)
            st.then(v.tensor_tensor(m0["xc"], m0["a"], m0["a"], ALU.mult))
            dve.wait_ge(rg_t, 4)
            v.scalar_tensor_tensor(out=m0["xc"], in0=m0["xc"], scalar=1.0, in1=m0["r"], op0=ALU.add, op1=ALU.mult
                                   ).then_inc(rg_m2, 1)
            dve.wait_ge(gelu_t, 1)
            st.then(v.scalar_tensor_tensor(out=gx, in0=gx, scalar=1.0, in1=ga, op0=ALU.add, op1=ALU.mult))
            dve.wait_ge(rg_m, 1)
            st.then(v.tensor_tensor(m0["i"], m0["i"], m0["xc"], ALU.mult))
            for m in range(4):
                st.then(v.tensor_tensor_scan(m0["r"][:, m, :], m0["a"][:, m, :], m0["i"][:, m, :], 0.0,
                                             ALU.mult, ALU.add))
            dve.wait_ge(rtab_out, 16)
            v.scalar_tensor_tensor(out=m0["y"][:, 0:4, :], in0=gx, scalar=0.5, in1=m0["r"], op0=ALU.mult,
                                   op1=ALU.mult).then_inc(ya_ready, 1)

            for n in range(NA + 3):
                if n < NA:
                    hd, N = n // NT, (n % NT + 1) * P
                    if n % NT == 0:
                        dve.wait_ge(strip_in[hd % 2], 16 * (hd // 2 + 1))
                        v.memset(m0["strip"][64:128, hd % 2, T - 64:T], -1e30).then_inc(strip_ready, 1)
                        dve.wait_ge(strip_ready, hd + 1)
                    wait_full(dve, ("S", n))
                    if n >= 3:
                        wait_full(dve, ("T", n - 3))
                    drains(v.tensor_tensor_reduce(m0["s"][:, n % 3, 0:N], bank(("S", n))[:, 0:N],
                                                  m0["strip"][:, hd % 2, T - N:T], 1.0, 0.0, ALU.add, ALU.max,
                                                  m0["mx"][:, n:n + 1]), ("S", n))
                if 1 <= n <= NA:
                    q = n - 1
                    N = (q % NT + 1) * P
                    dve.wait_ge(prob_exp, q + 1)
                    v.reciprocal(m0["rs"][:, q:q + 1], m0["sum"][:, q:q + 1]).then_inc(rsum_ready, 1)
                if n < NA:
                    wait_drained(dve, ("S", n))
                    v.tensor_scalar(m0["nmx"][:, n:n + 1], m0["mx"][:, n:n + 1], -1.0, None, ALU.mult
                                    ).then_inc(score_max, 1)
                if 1 <= n <= NA:
                    dve.wait_ge(rsum_ready, q + 1)
                    v.tensor_scalar(m0["s"][:, q % 3, 0:N], m0["s"][:, q % 3, 0:N], m0["rs"][:, q:q + 1], None,
                                    ALU.mult).then_inc(prob_ready, 1)
                if n >= 3:
                    q = n - 3
                    hd, i, lo = q // NT, q % NT, 64 * (q // NT % 2)
                    wait_full(dve, ("O", q))
                    drains(v.tensor_copy(m0["y"][lo:lo + 64, 4 + hd // 2, i * P:(i + 1) * P][:, ::-1],
                                         bank(("O", q))[lo:lo + 64, 0:P]), ("O", q))
            mixer_end(0)

            def route(l):
                lg, em, key, M0, M1, M = (me[k] for k in ("lg", "em", "key", "M0", "M1", "M"))
                g4, goh, ex, w, pos = me["g4"], me["goh"], me["ex"], me["w"], me["pos"]
                wt = lambda i: w[:, i, :]
                one = lambda a, n: a.unsqueeze(2).broadcast_to([P, NT, n])
                row = lambda a, n: a[:].unsqueeze(1).broadcast_to([P, NT, n])
                job = ("lg", l)
                if l == 0:
                    dve.wait_ge(made, 8)
                wait_full(dve, ("lgT", l))
                drains(v.tensor_copy(me["lgT"][0:NG + NE, :], bank(("lgT", l))[0:NG + NE, :]), ("lgT", l))
                wait_full(dve, job)
                drains(v.tensor_copy(lg, bank(job)[:, 0:256].rearrange("p (t n) -> p t n", t=NT)[:, :, 0:NG + NE]), job)
                wait_drained(dve, job)
                st.then(v.tensor_reduce(wt(0), lg[:, :, 0:NG], AX.X, ALU.max))
                st.then(v.tensor_tensor(g4, lg[:, :, 0:NG], one(wt(0), NG), ALU.is_equal))
                st.then(v.tensor_tensor(g4, g4, row(gkey, NG), ALU.mult))
                st.then(v.tensor_reduce(wt(1), g4, AX.X, ALU.max))
                st.then(v.tensor_tensor(goh, g4, one(wt(1), NG), ALU.is_equal))
                by_group = lambda a: a.rearrange("p t (g k) -> p t g k", g=NG)
                spread = lambda a: a.unsqueeze(3).broadcast_to([P, NT, NG, NPG])
                le = lg[:, :, NG:NG + NE]
                for t in range(NT):
                    sp4 = goh[:, t, :].unsqueeze(2).broadcast_to([P, NG, NPG])
                    ins = v.tensor_tensor(em[:, t, :].rearrange("p (g k) -> p g k", g=NG),
                                          le[:, t, :].rearrange("p (g k) -> p g k", g=NG), sp4, ALU.mult)
                st.then(ins)
                st.then(v.tensor_scalar(g4, goh, 1e30, -1e30, ALU.mult, ALU.add))
                for t in range(NT):
                    sp4 = g4[:, t, :].unsqueeze(2).broadcast_to([P, NG, NPG])
                    e4 = em[:, t, :].rearrange("p (g k) -> p g k", g=NG)
                    ins = v.tensor_tensor(e4, e4, sp4, ALU.add)
                st.then(ins)
                for k, dst in ((0, M0), (1, M1)):
                    st.then(v.tensor_reduce(wt(2 + k), em, AX.X, ALU.max))
                    st.then(v.tensor_tensor(key, em, one(wt(2 + k), NE), ALU.is_equal))
                    st.then(v.tensor_tensor(key, key, row(ekey, NE), ALU.mult))
                    st.then(v.tensor_reduce(wt(4), key, AX.X, ALU.max))
                    st.then(v.tensor_tensor(dst, key, one(wt(4), NE), ALU.is_equal))
                    if k == 0:
                        st.then(v.scalar_tensor_tensor(out=em, in0=M0, scalar=-1e31, in1=em, op0=ALU.mult, op1=ALU.add))
                st.then(v.tensor_tensor(M, M0, M1, ALU.add))
                Ms = me["Msum"]
                v.tensor_copy(Ms[:, 0, :], M[:, 0, :])
                v.tensor_tensor(Ms[:, 2, :], M[:, 1, :], M[:, 2, :], ALU.add)
                st.then(v.tensor_tensor(Ms[:, 1, :], M[:, 0, :], M[:, 1, :], ALU.add))
                v.tensor_tensor(Ms[:, 3, :], Ms[:, 2, :], M[:, 3, :], ALU.add)
                st.then(v.tensor_tensor(Ms[:, 2, :], Ms[:, 2, :], M[:, 0, :], ALU.add))
                v.tensor_tensor(Ms[:, 3, :], Ms[:, 3, :], M[:, 0, :], ALU.add).then_inc(one_hot, 1)
                st.then(v.tensor_tensor(ex[:, :, 0:NG], lg[:, :, 0:NG], one(wt(0), NG), ALU.subtract))
                v.tensor_tensor(ex[:, :, NG], wt(3), wt(2), ALU.subtract).then_inc(route_in, 1)
                job = ("pos", l)
                wait_full(dve, job)
                st.then(v.scalar_tensor_tensor(out=me["slots"], in0=bank(job)[:, 0:NT * NE].rearrange(
                    "p (t n) -> p t n", t=NT), scalar=1.0, in1=M, op0=ALU.add, op1=ALU.mult))
                st.then(v.tensor_scalar(me["slots"], me["slots"], -1.0, None, ALU.add))
                for e in range(2):
                    select(l, e, e)
                for k, Mk in ((0, M0), (1, M1)):
                    st.then(v.tensor_tensor(em, bank(job)[:, 0:NT * NE].rearrange("p (t n) -> p t n", t=NT), Mk, ALU.mult))
                    st.then(v.tensor_reduce(pos[:, k, :], em, AX.X, ALU.add))
                for k, Mk in ((0, M0), (1, M1)):
                    st.then(v.tensor_tensor(me["B"][:, k, :, :], Mk, one(tokval[:, k, :], NE), ALU.mult))
                    ins = v.tensor_tensor(me["A"][:, k, :, :], row(iota, CAP), one(pos[:, k, :], CAP), ALU.is_equal)
                    if k == 0:
                        st.then(ins)
                    else:
                        ins.then_inc(slots_hot, 1)
                drains(v.tensor_reduce(w[:, 5, 0:1], bank(job)[:, 256:256 + NE], AX.X, ALU.max), job)
                wait_drained(dve, job)
                v.tensor_scalar(flag[:, l:l + 1], w[:, 5, 0:1], CAP + 0.5, None, ALU.is_gt).then_inc(flag_ready, 1)
                turned(l, 0, 0)
                job = ("tab", l)
                wait_full(dve, job)
                tab = me["tab"][0:CAP, :, :]
                drains(v.tensor_copy(tab[:, 0, :], bank(job)[0:CAP, 0:NE]), job)
                wait_drained(dve, job)
                st.then(v.tensor_scalar(tab[:, 1, :], tab[:, 0, :], 0.0, OFF, ALU.is_equal, ALU.mult))
                st.then(v.scalar_tensor_tensor(out=tab[:, 1, :], in0=tab[:, 0, :], scalar=-1.0, in1=tab[:, 1, :],
                                               op0=ALU.add, op1=ALU.add))
                v.tensor_copy(ri[:], tab[:, 1, :]).then_inc(table_ready, 1)
                dve.wait_ge(route_exp, l + 1)
                st.then(v.tensor_reduce(wt(6), ex[:, :, 0:NG], AX.X, ALU.add))
                st.then(v.tensor_scalar(wt(7), ex[:, :, NG], 1.0, None, ALU.add))
                st.then(v.tensor_tensor(wt(6), wt(6), wt(7), ALU.mult))
                st.then(v.reciprocal(gates[:, 0, :], wt(6)))
                st.then(v.tensor_tensor(gates[:, 1, :], gates[:, 0, :], ex[:, :, NG], ALU.mult))

            def times_gain(l, dst):
                g8 = at["ffn_g"][:, l * NC:(l + 1) * NC].unsqueeze(2).broadcast_to([P, NC, CAP])
                return v.tensor_tensor(dst.rearrange("p (c t) -> p c t", c=NC),
                                       ps[BX][:].rearrange("p (c t) -> p c t", c=NC), g8, ALU.mult)

            def select(l, e, j):
                if isinstance(e, int) and e < 2:
                    column = me["slots"][:, :, e]
                else:
                    column = me["slot"][:, j, :]
                    dve.wait_ge(col_ready, e + (l * (NE - 2) - 1))
                    dve.wait_ge(filled[BR], e + (moe_base[l][BR] - 1))
                v.tensor_tensor(me["sel"][:, j, :].rearrange("p (t s) -> p t s", t=NT),
                                iota[:].unsqueeze(1).broadcast_to([P, NT, CAP]),
                                column.unsqueeze(2).broadcast_to([P, NT, CAP]), ALU.is_equal
                                ).then_inc(sel_ready, 1)

            def turned(l, e, j):
                base = moe_base[l]
                dve.wait_ge(filled[BX], e + (base[BX] + 1))
                if not (isinstance(e, int) and e < 2):
                    dve.wait_ge(filled[BG], e + (base[BG] - 1))
                g8 = at["ffn_g"][:, l * NC:(l + 1) * NC].rearrange("p (z c) -> p c z", z=2)
                v.tensor_tensor(me["xgT"][:, j, :].rearrange("p (z c t) -> p c z t", z=2, c=4),
                                ps[BX][:].rearrange("p (c z t) -> p c z t", c=4, z=2),
                                g8.unsqueeze(3).broadcast_to([P, 4, 2, CAP]), ALU.mult).then_inc(drained[BX], 1)

            def hidden_rows(j):
                return v.tensor_tensor(me["hrow"][0:CAP, :], me["silu"][64:128, j, :], ps[BG][64:128, :], ALU.mult)

            def dve_expert(l, e, k, j, ahead=2):
                base = moe_base[l]
                dve.wait_ge(silu_ready, e + (l * NE + 1))
                if not (isinstance(e, int) and e == 0):
                    dve.wait_ge(filled[BH], e + base[BH])
                hidden_rows(j).then_inc(drained[BG], 1)
                if ahead >= 1:
                    turned(l, e + 1, 1 - j)
                if ahead >= 2:
                    select(l, e + 2, j)
                dve.wait_ge(filled[BH], e + (base[BH] + 1))
                if not (isinstance(e, int) and e == 0):
                    dve.wait_ge(filled[BY], e + base[BY])
                v.tensor_copy(me["hT"], ps[BH][:, 0:FC * CAP]).then_inc(drained[BH], 1)
                dve.wait_ge(half_out, e + (l * NE + 1))
                if not (isinstance(k, int) and k == 0):
                    dve.wait_ge(scattered[j], k * 16 + 16 * l * (NE // 2))
                v.tensor_copy(me["rows"][0:CAP, 2 + j, 512:1024], ps[BY][64:128, :]).then_inc(drained[BY], 1)

            def more_blocks(l):
                dve.wait_ge(flag_ready, l + 1)
                more = dve.value_load(flag[0:1, l:l + 1], min_val=0, max_val=1)
                o, per_e = ov[l], BLOCKS - 1
                s2 = o["step"]
                with dve.If(more > 0):
                    dve.wait_ge(o["pe"], 1)
                    tab = me["tab"][0:CAP, :, :]
                    with dve.Fori(0, per_e) as b:
                        so = Steps(dve, s2)
                        so.base = b * 5
                        so.then(v.tensor_scalar(iota[:], iota[:], float(CAP), None, ALU.add))
                        for k in range(2):
                            ins = v.tensor_tensor(me["A"][:, k, :, :], iota[:].unsqueeze(1).broadcast_to([P, NT, CAP]),
                                                  me["pos"][:, k, :].unsqueeze(2).broadcast_to([P, NT, CAP]),
                                                  ALU.is_equal)
                        ins.then_inc(o["tab"], 1)
                        dve.wait_ge(o["tabpe"], b + 1)
                        so.then(v.tensor_copy(tab[:, 0, :], ps[6][0:CAP, 0:NE]))
                        so.then(v.tensor_scalar(tab[:, 1, :], tab[:, 0, :], 0.0, OFF, ALU.is_equal, ALU.mult))
                        so.then(v.scalar_tensor_tensor(out=tab[:, 1, :], in0=tab[:, 0, :], scalar=-1.0,
                                                       in1=tab[:, 1, :], op0=ALU.add, op1=ALU.add))
                        so.then(v.tensor_scalar(tab[:, 2, :], tab[:, 0, :], T + 0.5, -float(T), ALU.is_gt, ALU.mult))
                        v.tensor_copy(rio[:, bass.ds(b * NE, NE)], tab[:, 1, :])
                        v.tensor_tensor(xio[:, bass.ds(b * NE, NE)], tab[:, 1, :], tab[:, 2, :], ALU.add
                                        ).then_inc(o["tab"], 1)
                        dve.wait_ge(o["tab"], b * 2 + 2)
                    v.tensor_scalar(iota[:], iota[:], -float(CAP * per_e), None, ALU.add).then_inc(s2, 1)
                    dve.wait_ge(s2, per_e * 5 + 1)
                    with dve.Fori(0, NE * per_e) as n:
                        dve.wait_ge(o["pe"], n * 4 + 2)
                        times_gain(l, me["xgT"][:, 0, :]).then_inc(o["dve"], 1)
                        dve.wait_ge(o["act"], n * 2 + 1)
                        hidden_rows(0).then_inc(o["dve"], 1)
                        dve.wait_ge(o["pe"], n * 4 + 4)
                        v.tensor_copy(me["hT"], ps[BH][:, 0:FC * CAP]).then_inc(o["dve"], 1)
                        dve.wait_ge(o["act"], n * 2 + 2)
                        v.tensor_copy(me["rows"][0:CAP, 2, 512:1024], ps[BY][64:128, :]).then_inc(o["dve"], 1)

            def combine(l, t):
                dve.wait_ge(yrow_in[t], 32 * (l + 1))
                for k in range(2):
                    v.scalar_tensor_tensor(out=h[:, t, :], in0=yrows[:, 2 * t + k, :], scalar=gates[:, k, t:t + 1],
                                           in1=h[:, t, :], op0=ALU.mult, op1=ALU.add).then_inc(h_ready, 1)
                    dve.wait_ge(h_ready, l * 2 * NT + 2 * t + k + 1)

            def final(t):
                norm_col(4, t)
                dve.wait_ge(rstd_ready, 4 * NT + t + 1)
                dve.wait_ge(final_in, 16)
                v.scalar_tensor_tensor(out=xh[:, t, :], in0=h[:, t, :], scalar=rstd[:, 4, t:t + 1], in1=me["fin_g"],
                                       op0=ALU.mult, op1=ALU.mult).then_inc(out_ready, 1)

            def moe(l):
                route(l)
                dve_expert(l, 0, 0, 0)
                dve_expert(l, 1, 0, 1)
                with dve.Fori(1, NE // 2 - 1) as i:
                    dve_expert(l, i * 2, i, 0)
                    dve_expert(l, i * 2 + 1, i, 1)
                dve_expert(l, NE - 2, NE // 2 - 1, 0, ahead=1)
                dve_expert(l, NE - 1, NE // 2 - 1, 1, ahead=0)
                more_blocks(l)
                for t in range(NT + 2):
                    if t < NT:
                        combine(l, t)
                    if 1 <= t <= NT:
                        if l == 0:
                            norm_col(2, t - 1)
                            norm_rows(2, t - 1)
                        else:
                            final(t - 1)
                    if t >= 2 and l == 0:
                        turned_rows(2, t - 2)

            dve.wait_ge(lb_exp, 1)
            st.then(v.tensor_tensor(lbt[:, 0, :], lbt[:, 2, :], lbt[:, 3, :], ALU.add))
            st.then(v.reciprocal(lbt[:, 0, :], lbt[:, 0, :]))
            st.then(v.tensor_tensor(lb[:], lbt[:, 2, :], lbt[:, 0, :], ALU.mult))
            st.then(v.tensor_scalar(oml[:], lb[:], -1.0, 1.0, ALU.mult, ALU.add))
            moe(0)

            def sub_level(G, L):
                m = P >> L
                nb = T // (2 * m)
                b = m1["b"][:, G % 2, :].rearrange("p (a b) -> p a b", a=nb)
                e = m1["e"][:, L % 2, :].rearrange("p (a b) -> p a b", a=nb)
                mid = b[:, :, m - 1:m].broadcast_to([P, nb, m])
                if L == 1:
                    dve.wait_ge(b_ready, G + 1)
                last = G * LEVELS + L - 2 if L > 2 else G * LEVELS + (0 if L == 1 else -1)
                if last > 0:
                    dve.wait_ge(qk_ready, last)
                v.tensor_tensor(e[:, :, 0:m], mid, b[:, :, 0:m], ALU.subtract)
                v.tensor_tensor(e[:, :, m:2 * m], b[:, :, m:2 * m], mid, ALU.subtract).then_inc(e_sub, 1)

            def take_level(G, L):
                job = ("lev", G, L)
                src = bank(job)[:].rearrange("p (a b) -> p a b", a=NT)
                dst = m1["attn"][:, G % 2, :].rearrange("p (a b) -> p a b", a=NT)
                wait_full(dve, job)
                if L == 0:
                    if G >= 2:
                        wait_full(dve, ("o", G - 2))
                    drains(v.tensor_tensor(dst, src, ident[:].unsqueeze(1).broadcast_to([P, NT, P]), ALU.mult), job)
                else:
                    wait_drained(dve, ("lev", G, L - 1))
                    drains(v.copy_predicated(dst, masks[:, L - 1, :].bitcast(U32).unsqueeze(1).broadcast_to([P, NT, P]), src), job)

            for H in range(HEADS_C + 2):
                new, G, O = H < HEADS_C, H - 1, H - 2
                core, outp = 0 <= G < HEADS_C, O >= 0
                if core:
                    sub_level(G, 1)
                    sub_level(G, 2)
                    b3 = m1["b"][:, G % 2, 0:3 * P].rearrange("p (a b) -> p a b", a=3)
                    if G > 0:
                        wait_full(dve, ("khT", G - 1))
                    v.tensor_tensor(m1["dl"], b3[:, :, P - 1:P].broadcast_to([P, 3, P]), b3, ALU.subtract
                                    ).then_inc(dl_sub, 1)
                    take_level(G, 0)
                if new:
                    wait_drained(dve, ("c", H, 0))
                    v.tensor_scalar(m1["f"], m1["f"], oml[:, H:H + 1], lb[:, H:H + 1], ALU.mult, ALU.add
                                    ).then_inc(f_ready, 1)
                if core:
                    sub_level(G, 3)
                    take_level(G, 1)
                    sub_level(G, 4)
                    take_level(G, 2)
                if new:
                    dve.wait_ge(lf_ready, H + 1)
                    b = m1["b"][:, H % 2, :]
                    v.tensor_tensor_scan(b, keep[:], b, 0.0, ALU.mult, ALU.add).then_inc(b_ready, 1)
                if outp:
                    dve.wait_ge(rs_ready, O + 1)
                    wait_full(dve, ("o", O))
                    drains(v.tensor_tensor(m1["rs"], bank(("o", O))[:], m1["rs"], ALU.mult), ("o", O))
                    wait_drained(dve, ("o", O))
                    dve.wait_ge(sgg_ready, O + 1)
                    v.tensor_tensor(m1["y"][:, O, :], m1["rs"], m1["sg"][:, O % 2, :], ALU.mult).then_inc(y_ready, 1)
                if core:
                    sub_level(G, 5)
                    take_level(G, 3)
                    sub_level(G, 6)
                    take_level(G, 4)
                    job = ("dst", G)
                    wait_full(dve, job)
                    dve.wait_ge(eb_ready, G + 1)
                    if G >= 2:
                        wait_full(dve, ("o", G - 2))
                    stt, src = m1["st"][:, G % 2, :], bank(job)
                    st.then(v.tensor_copy(stt[:, 0:P], src[:, 0:P]))
                    st.then(v.scalar_tensor_tensor(out=stt[:, P:2 * P], in0=stt[:, 0:P],
                                                   scalar=m1["eb"][:, 2 * P - 1:2 * P], in1=src[:, P:2 * P],
                                                   op0=ALU.mult, op1=ALU.add))
                    drains(v.scalar_tensor_tensor(out=stt[:, 2 * P:3 * P], in0=stt[:, P:2 * P],
                                                  scalar=m1["eb"][:, 3 * P - 1:3 * P], in1=src[:, 2 * P:3 * P],
                                                  op0=ALU.mult, op1=ALU.add), job)
                    sub_level(G, 7)
                    take_level(G, 5)
                    take_level(G, 6)
                    take_level(G, 7)
            mixer_end(1)
            moe(1)

    return nc


def kernel(**inputs):
    import numpy as _np
    import concourse.bacc as _bacc
    from concourse import mybir as _mybir
    from concourse.bass_utils import run_bass_kernel_spmd as _run

    a = {k: _np.asarray(v) for k, v in inputs.items()}

    def chunks(vector):
        return vector.reshape(-1, P).T

    cols = _np.concatenate(
        [chunks(a["norm_mix_g"][l]) for l in range(2)] + [chunks(a["norm_ffn_g"][l]) for l in range(2)]
        + [a["ab_conv_w"][0].reshape(CONV, 4, P).transpose(2, 1, 0).reshape(P, 4 * CONV)]
        + [chunks(a[k][0]) for k in ("ab_conv_b", "rg_b_a", "rg_b_x", "rg_lambda")]
        + [chunks(a["c_lb_logits"][i]) for i in range(2)] + [chunks(a["c_norm_g"][0])], axis=1)
    router = _np.concatenate([a["moe_router_group"], a["moe_router_expert"]], axis=2)
    router = router.reshape(2, NC, P, NG + NE).transpose(2, 0, 1, 3).reshape(P, -1)
    c_in = a["c_w_in"][0].reshape(NC, P, 4, HEADS_C, P)[:, :, [1, 0, 2, 3]].transpose(3, 1, 0, 2, 4)
    feeds = {
        "x": a["x"], "cols": cols, "final_g": a["norm_final_g"], "ab_w_in": a["ab_w_in"], "rg_w_a": a["rg_w_a"],
        "rg_w_x": a["rg_w_x"], "bias_rev": a["attn_rel_bias"][0][:, ::-1], "ab_w_out": a["ab_w_out"],
        "c_w_in": c_in.reshape(HEADS_C, P, -1), "c_w_out": a["c_w_out"], "router": router,
        "w_gate": a["moe_w_gate"], "w_up": a["moe_w_up"], "w_down": a["moe_w_down"],
    }
    nc = _bacc.Bacc("TRN2", target_bir_lowering=False, num_devices=1)
    arrays, args = {}, []
    for name, value in feeds.items():
        value = _np.ascontiguousarray(value)
        arrays[f"in_{name}_dram"] = value
        args.append(nc.dram_tensor(f"in_{name}_dram", value.shape, _mybir.dt.from_np(value.dtype),
                                   kind="ExternalInput").ap())
    out = nc.dram_tensor("out_dram", (1, T, D), F32, kind="ExternalOutput").ap()
    trunk(nc, *args, out)
    r = _run(nc, [arrays], core_ids=[0])
    return r.results[0]["out_dram"]
```
